# Optimizing a Trainium2 kernel written in Bass

```python
import math
import jax, jax.numpy as jnp
from jax import lax
import numpy as np

D_MODEL = 1024
BATCH = 1
SEQ = 2048
DEPTH = 1

CHUNK = 64
Q_BLOCK = 128
N_MIXERS = 3
D_FF = 4 * D_MODEL
EPS = 1e-6

A_HEADS = 8
A_HEAD_DIM = D_MODEL // (2 * A_HEADS)
A_V_DIM = 2 * A_HEAD_DIM

POOL_WINDOWS = (2, 4, 8, 16)
POOL_GROUP = D_MODEL // len(POOL_WINDOWS)

C_HEADS = 8
C_HEAD_DIM = D_MODEL // C_HEADS
C_KV_HEADS = 2
IDX_HEADS = 8
IDX_DIM = 64
TOPK_MAX = 256
C_SPLIT_SIZES = (C_HEADS * C_HEAD_DIM, C_KV_HEADS * C_HEAD_DIM, C_KV_HEADS * C_HEAD_DIM,
                 IDX_HEADS * IDX_DIM, IDX_DIM, IDX_HEADS)
C_IN = sum(C_SPLIT_SIZES)

kernel_name = "hybrid_diffattn_pool_dsa_trunk"

def _n_layers_of(mixer):
    return len([i for i in range(DEPTH) if i % N_MIXERS == mixer])

def rms_norm(x, g):
    xf = x.astype(jnp.float32)
    y = xf * lax.rsqrt(jnp.mean(xf * xf, axis=-1, keepdims=True) + EPS)
    return (y * g.astype(jnp.float32)).astype(x.dtype)

def diff_attention(h, w_in, q_g, k_g, lq1, lk1, lq2, lk2, sub_g, w_out, lambda_init):
    B, S, _ = h.shape
    H, Dh = A_HEADS, A_HEAD_DIM
    q, k, v = jnp.split(h @ w_in, 3, axis=-1)
    q = rms_norm(q.reshape(B, S, H, 2, Dh), q_g)
    k = rms_norm(k.reshape(B, S, H, 2, Dh), k_g)
    v = v.reshape(B, S, H, A_V_DIM)
    f32 = jnp.float32
    lam = (jnp.exp(jnp.sum(lq1.astype(f32) * lk1.astype(f32)))
           - jnp.exp(jnp.sum(lq2.astype(f32) * lk2.astype(f32))) + lambda_init)
    nb = S // Q_BLOCK
    qb = q.reshape(B, nb, Q_BLOCK, H, 2, Dh).transpose(1, 0, 2, 3, 4, 5)
    key_chunk = jnp.arange(S) // CHUNK
    scale = Dh ** -0.5

    def block(args):
        qi, bi = args
        q_chunk = (bi * Q_BLOCK + jnp.arange(Q_BLOCK)) // CHUNK
        mask = key_chunk[None, :] <= q_chunk[:, None]
        s = jnp.einsum('bqhmd,bshmd->bhmqs', qi, k).astype(f32) * scale
        s = jnp.where(mask, s, -jnp.inf)
        p = jax.nn.softmax(s, axis=-1)
        pd = (p[:, :, 0] - lam * p[:, :, 1]).astype(v.dtype)
        return jnp.einsum('bhqs,bshe->bqhe', pd, v)

    o = lax.map(block, (qb, jnp.arange(nb)))
    o = o.transpose(1, 0, 2, 3, 4).reshape(B, S, H, A_V_DIM)
    o = rms_norm(o, sub_g) * (1.0 - lambda_init)
    return o.reshape(B, S, H * A_V_DIM) @ w_out

def pool_mixer(h, w_group, scale):
    B, S, D = h.shape
    hf = h.astype(jnp.float32)
    cs = jnp.pad(jnp.cumsum(hf, axis=1), ((0, 0), (1, 0), (0, 0)))
    t = jnp.arange(S)
    outs = []
    for g, w in enumerate(POOL_WINDOWS):
        c = cs[:, :, g * POOL_GROUP:(g + 1) * POOL_GROUP]
        prev = jnp.pad(c, ((0, 0), (w - 1, 0), (0, 0)))[:, :S]
        count = jnp.minimum(t + 1, w).astype(jnp.float32)
        mean = (c[:, 1:] - prev) / count[None, :, None]
        outs.append(mean - hf[:, :, g * POOL_GROUP:(g + 1) * POOL_GROUP])
    pooled = jnp.stack(outs, axis=2).astype(h.dtype)
    y = jnp.einsum('bsgc,gce->bsge', pooled, w_group).reshape(B, S, D)
    return y * scale

def dsa_attention(h, w_in, q_g, k_g, w_out):
    B, S, _ = h.shape
    H, G, Dh = C_HEADS, C_KV_HEADS, C_HEAD_DIM
    R = H // G
    f32 = jnp.float32
    offsets = list(np.cumsum(C_SPLIT_SIZES)[:-1])
    q, k, v, iq, ik, iw = jnp.split(h @ w_in, offsets, axis=-1)
    q = rms_norm(q.reshape(B, S, G, R, Dh), q_g)
    k = rms_norm(k.reshape(B, S, G, Dh), k_g)
    v = v.reshape(B, S, G, Dh)
    iq = iq.reshape(B, S, IDX_HEADS, IDX_DIM)
    iw = iw * (IDX_HEADS ** -0.5)
    topk = min(TOPK_MAX, S // 4)
    nb = S // Q_BLOCK
    qb = q.reshape(B, nb, Q_BLOCK, G, R, Dh).transpose(1, 0, 2, 3, 4, 5)
    iqb = iq.reshape(B, nb, Q_BLOCK, IDX_HEADS, IDX_DIM).transpose(1, 0, 2, 3, 4)
    iwb = iw.reshape(B, nb, Q_BLOCK, IDX_HEADS).transpose(1, 0, 2, 3)
    key_chunk = jnp.arange(S) // CHUNK

    def block(args):
        qi, iqi, iwi, bi = args
        q_chunk = (bi * Q_BLOCK + jnp.arange(Q_BLOCK)) // CHUNK
        admissible = key_chunk[None, :] <= q_chunk[:, None]
        logits = jnp.einsum('bqhd,bsd->bqhs', iqi, ik).astype(f32) * (IDX_DIM ** -0.5)
        score = jnp.einsum('bqh,bqhs->bqs', iwi.astype(f32), jax.nn.relu(logits))
        score = jnp.where(admissible[None], score, -jnp.inf)
        _, idx = lax.top_k(score, topk)
        valid = (idx // CHUNK) <= q_chunk[None, :, None]
        k_sel = jax.vmap(lambda kk, ii: kk[ii])(k, idx)
        v_sel = jax.vmap(lambda vv, ii: vv[ii])(v, idx)
        s = jnp.einsum('bqgrd,bqjgd->bqgrj', qi, k_sel).astype(f32) * (Dh ** -0.5)
        s = jnp.where(valid[:, :, None, None, :], s, -jnp.inf)
        p = jax.nn.softmax(s, axis=-1).astype(v.dtype)
        return jnp.einsum('bqgrj,bqjgd->bqgrd', p, v_sel)

    o = lax.map(block, (qb, iqb, iwb, jnp.arange(nb)))
    o = o.transpose(1, 0, 2, 3, 4, 5).reshape(B, S, H * Dh)
    return o @ w_out

def setup_inputs(seed: int = 0) -> dict:
    key = jax.random.key(seed)
    ks = jax.random.split(key, 24)
    f32 = jnp.float32
    nA, nB, nC = _n_layers_of(0), _n_layers_of(1), _n_layers_of(2)

    def w(k, shape, fan_in, gain=1.0):
        return jax.random.normal(k, shape, f32) * (gain * fan_in ** -0.5)

    def g(k, shape):
        return 1.0 + 0.02 * jax.random.normal(k, shape, f32)

    def lam(k, shape):
        return 0.1 * jax.random.normal(k, shape, f32)

    return {
        "x": jax.random.normal(ks[0], (BATCH, SEQ, D_MODEL), f32),
        "norm1_g": g(ks[1], (DEPTH, D_MODEL)),
        "norm2_g": g(ks[2], (DEPTH, D_MODEL)),
        "a_w_in": w(ks[3], (nA, D_MODEL, 3 * D_MODEL), D_MODEL),
        "a_q_norm_g": g(ks[4], (nA, A_HEAD_DIM)),
        "a_k_norm_g": g(ks[5], (nA, A_HEAD_DIM)),
        "a_lambda_q1": lam(ks[6], (nA, A_HEAD_DIM)),
        "a_lambda_k1": lam(ks[7], (nA, A_HEAD_DIM)),
        "a_lambda_q2": lam(ks[8], (nA, A_HEAD_DIM)),
        "a_lambda_k2": lam(ks[9], (nA, A_HEAD_DIM)),
        "a_subln_g": g(ks[10], (nA, A_V_DIM)),
        "a_w_out": w(ks[11], (nA, A_HEADS * A_V_DIM, D_MODEL), A_HEADS * A_V_DIM, 0.5),
        "b_w_group": w(ks[12], (nB, len(POOL_WINDOWS), POOL_GROUP, POOL_GROUP), POOL_GROUP),
        "b_scale": g(ks[13], (nB, D_MODEL)),
        "c_w_in": w(ks[14], (nC, D_MODEL, C_IN), D_MODEL),
        "c_q_norm_g": g(ks[15], (nC, C_HEAD_DIM)),
        "c_k_norm_g": g(ks[16], (nC, C_HEAD_DIM)),
        "c_w_out": w(ks[17], (nC, C_HEADS * C_HEAD_DIM, D_MODEL), C_HEADS * C_HEAD_DIM, 0.5),
        "mlp_w1": w(ks[18], (DEPTH, D_MODEL, D_FF), D_MODEL),
        "mlp_w2": w(ks[19], (DEPTH, D_FF, D_MODEL), D_FF, 0.5),
    }

def reference(x, norm1_g, norm2_g, a_w_in, a_q_norm_g, a_k_norm_g, a_lambda_q1, a_lambda_k1,
              a_lambda_q2, a_lambda_k2, a_subln_g, a_w_out, b_w_group, b_scale, c_w_in,
              c_q_norm_g, c_k_norm_g, c_w_out, mlp_w1, mlp_w2):
    h = x
    for i in range(DEPTH):
        m, j = i % N_MIXERS, i // N_MIXERS
        u = rms_norm(h, norm1_g[i])
        if m == 0:
            lambda_init = 0.8 - 0.6 * math.exp(-0.3 * i)
            y = diff_attention(u, a_w_in[j], a_q_norm_g[j], a_k_norm_g[j], a_lambda_q1[j],
                               a_lambda_k1[j], a_lambda_q2[j], a_lambda_k2[j], a_subln_g[j],
                               a_w_out[j], lambda_init)
        elif m == 1:
            y = pool_mixer(u, b_w_group[j], b_scale[j])
        else:
            y = dsa_attention(u, c_w_in[j], c_q_norm_g[j], c_k_norm_g[j], c_w_out[j])
        h = h + y
        u = rms_norm(h, norm2_g[i])
        h = h + jnp.square(jax.nn.relu(u @ mlp_w1[i])) @ mlp_w2[i]
    return h


_drawn_inputs = setup_inputs


def setup_inputs(seed=0):
    import zlib

    import numpy as np

    out = dict(_drawn_inputs(seed))
    spreads = {}
    factors = {'norm1_g': 3.651,
     'norm2_g': 4.854,
     'a_q_norm_g': 7.743,
     'a_k_norm_g': 6.673,
     'a_lambda_q1': 5.427,
     'a_lambda_k2': 8.0,
     'a_subln_g': 6.43}
    for name, (base, spread) in spreads.items():
        noise = np.random.default_rng([zlib.crc32(name.encode()), seed]).standard_normal(out[name].shape)
        drawn = base * np.exp(spread * noise) if base else spread * noise
        out[name] = __import__('jax').numpy.asarray(drawn.astype(out[name].dtype))
    for name, factor in factors.items():
        out[name] = (out[name] * factor).astype(out[name].dtype)
    return out
```

```python
from contextlib import ExitStack

import concourse.bass as bass
from concourse import mybir

F32 = mybir.dt.float32
F32R = mybir.dt.float32r
BF16 = mybir.dt.bfloat16
ACT = mybir.ActivationFunctionType
ALU = mybir.AluOpType
AX = mybir.AxisListType

P = 128
S, D, DFF = 2048, 1024, 4096
H, DH = 8, 64
HD = 2 * DH
NT = S // P
KT = D // P
HALF = KT // 2
BANK = 512
TPB = BANK // P
EPS = 1e-6
SCALE = DH ** -0.5
LAMBDA_INIT = 0.2
MASKED = -1e30



def banks_of(j):
    return (NT - 1 - j) // TPB + 1


def groups_before(j):
    return sum(banks_of(i) for i in range(j))


def bank_order(j):
    return list(reversed(range(banks_of(j))))


def bank_width(j, bank):
    return min(BANK, (NT - j) * P - bank * BANK)


GROUPS = groups_before(NT)
SCORED = 2 * GROUPS


def score_index(j, m, n):
    return 2 * groups_before(j) + m * banks_of(j) + n


def turn_order(projecting):
    order = []
    for j in range(NT + 1):
        order += [("p", j - 1, n) for n in range(banks_of(j - 1) if j else 0)]
        if projecting and j:
            order.append(("qk", j - 1))
    return order


def attention_steps(nc, x, norm1_g, w_in, q_g, k_g, lambdas, o_dram):
    with ExitStack() as ctx:
        def sb(name, shape, dt=F32):
            return ctx.enter_context(nc.sbuf_tensor(name, shape, dt))

        def ps(name, shape):
            return ctx.enter_context(nc.psum_tensor(name, shape, F32))

        def sem(name):
            return ctx.enter_context(nc.semaphore(name))

        u_t = sb("u_t", [P, NT, KT, P])
        u_hi = sb("u_hi", [P, KT, P], F32R)
        u_lo = sb("u_lo", [P, KT, P], F32R)
        w_raw = sb("w_raw", [P, 2, 2, 3, HD])
        w_hi = sb("w_hi", [P, KT, 3 * HD], F32R)
        w_lo = sb("w_lo", [P, KT, 3 * HD], F32R)
        q_s = sb("q_s", [P, 2, S], F32R)
        k_hi = sb("k_hi", [P, 2, S], F32R)
        k_lo = sb("k_lo", [P, 2, S], F32R)
        v_s = sb("v_s", [P, NT, 2 * HD], F32R)
        p_all = sb("p_all", [P, 3, S])
        p1 = p_all[:, 2, :]
        pt_hi = sb("pt_hi", [P, 2, BANK], F32R)
        pt_lo = sb("pt_lo", [P, 2, BANK], F32R)
        qk_sq = sb("qk_sq", [P, 4 * DH])
        qk_ss = sb("qk_ss", [P, 4])
        qk_var = sb("qk_var", [P, 4])
        qk_rs = sb("qk_rs", [P, 4])
        qk_nat = sb("qk_nat", [P, 4, 2, DH])
        ident = sb("ident", [P, P])
        mask_l = sb("mask_l", [P, P], BF16)
        mask_r = sb("mask_r", [P, DH], BF16)
        g_q = sb("g_q", [P, 1])
        g_k = sb("g_k", [P, 1])
        lam_v = sb("lam_v", [P, 4, DH])
        lam_w = sb("lam_w", [P, 2, DH])
        lam_s = sb("lam_s", [P, 2])
        lam_e = sb("lam_e", [P, 2])
        lam_d = sb("lam_d", [P, 1])
        neg_lam = sb("neg_lam", [P, 1])
        minus_half = sb("minus_half", [P, 4])
        eps = sb("eps", [P, 4])
        mx = sb("mx", [P, 2, 2, TPB])
        m_all = sb("m_all", [P, 2, 2])
        nbias = sb("nbias", [P, 2, 2])
        z_part = sb("z_part", [P, 2, 2, TPB])
        z = sb("z", [P, 2, 2])
        rz = sb("rz", [P, 2, 2])
        neg_c = sb("neg_c", [P, 2])
        o_tmp = sb("o_tmp", [P, 2, HD])
        o_sum = sb("o_sum", [P, 2, HD])
        o_sq = sb("o_sq", [P, HD])
        o_ss = sb("o_ss", [P, 2])
        o_var = sb("o_var", [P, 2])
        o_rs = sb("o_rs", [P, 2])
        o_n = sb("o_n", [P, 2, HD])
        x_ss = sb("x_ss", [P, 2])
        x_var = sb("x_var", [P, 2])
        x_rs = sb("x_rs", [P, 2])
        x_in = p_all[:, 0, :].rearrange("p (a d) -> p a d", a=2)
        u_nat = p_all[:, 1, :].rearrange("p (a d) -> p a d", a=2)
        g1_row = p_all[:, 2, 0:D]
        x_junk = p_all[:, 2, D:2 * D]

        scores = ps("scores", [P, 4, BANK])
        turn = ps("turn", [P, 2, BANK])
        o_acc = ps("o_acc", [P, BANK])
        proj = ps("proj", [P, BANK])

        consts_loaded, ident_set, consts_set = sem("consts_loaded"), sem("ident_set"), sem("consts_set")
        lam_step = sem("lam_step")
        x_loaded = [sem("x_loaded0"), sem("x_loaded1")]
        x_squared, x_var_set, x_rs_set = sem("x_squared"), sem("x_var_set"), sem("x_rs_set")
        u_normed, u_turned, u_kept = sem("u_normed"), sem("u_turned"), sem("u_kept")
        w_loaded = [sem("w_loaded0"), sem("w_loaded1")]
        w_hi_set, w_lo_set = sem("w_hi_set"), sem("w_lo_set")
        u_hi_set, u_lo_set = sem("u_hi_set"), sem("u_lo_set")
        proj_half = sem("proj_half")
        qk_squared, qk_summed, qk_var_set, qk_rs_set = (
            sem("qk_squared"), sem("qk_summed"), sem("qk_var_set"), sem("qk_rs_set"))
        v_hi_set, v_lo_set, qk_normed, qk_turned = (
            sem("v_hi_set"), sem("v_lo_set"), sem("qk_normed"), sem("qk_turned"))
        q_hi_set, k_hi_set, q_lo_set, k_lo_set = (
            sem("q_hi_set"), sem("k_hi_set"), sem("q_lo_set"), sem("k_lo_set"))
        scored, bank_max, row_max, bias_set, exp_done = (
            sem("scored"), sem("bank_max"), sem("row_max"), sem("bias_set"), sem("exp_done"))
        z_summed, z_inverted, c_set, combined = (
            sem("z_summed"), sem("z_inverted"), sem("c_set"), sem("combined"))
        p_turned, pt_hi_set, pt_lo_set, pv_done = (
            sem("p_turned"), sem("pt_hi_set"), sem("pt_lo_set"), sem("pv_done"))
        o_low_set, o_summed, o_squared, o_var_set, o_rs_set, o_normed = (
            sem("o_low_set"), sem("o_summed"), sem("o_squared"), sem("o_var_set"),
            sem("o_rs_set"), sem("o_normed"))
        o_stored = [sem("o_stored0"), sem("o_stored1")]

        w_view = w_in.rearrange("(kt p) (s c) -> p kt s c", p=P, s=3)

        def load_weights(sp, hp):
            cols = bass.ds(hp * HD if isinstance(hp, int) else sp.snap(hp * HD), HD)
            for n in range(4):
                if not (isinstance(hp, int) and hp == 0 and n < 2):
                    sp.wait_ge(w_lo_set, hp * 4 + n - 1)
                for s in range(3):
                    sp.dma_start(w_raw[:, n % 2, :, s, :],
                                 w_view[:, 2 * n:2 * n + 2, s, cols])\
                      .then_inc(w_loaded[n % 2], 16)

        def raw_piece(n):
            return w_raw[:, n % 2].rearrange("p a s c -> p (a s c)")

        def w_piece(w, n):
            return w[:, 2 * n:2 * n + 2, :].rearrange("p a c -> p (a c)")

        def act_split_weights(act, hp):
            act.wait_ge(proj_half, hp * 2 * NT)
            for n in range(4):
                act.wait_ge(w_loaded[n % 2], (hp * 2 + n // 2 + 1) * 48)
                act.activation(w_piece(w_hi, n), raw_piece(n), ACT.Copy).then_inc(w_hi_set, 1)

        def pool_split_weights(pool, hp):
            for n in range(4):
                pool.wait_ge(w_hi_set, hp * 4 + n + 1)
                pool.tensor_tensor(w_piece(w_lo, n), raw_piece(n), w_piece(w_hi, n).bitcast(F32), ALU.subtract)\
                    .then_inc(w_lo_set, 1)

        def act_split_u(act, hp, j, halves=(0, 1)):
            t, n = NT - 1 - j, hp * NT + j
            for half in halves:
                kts = slice(half * HALF, (half + 1) * HALF)
                if not (isinstance(hp, int) and hp == 0 and j == 0):
                    act.wait_ge(proj_half, 2 * n + half - 1)
                act.activation(u_hi[:, kts, :], u_t[:, t, kts, :], ACT.Copy).then_inc(u_hi_set, 1)

        def pool_split_u(pool, hp, j):
            t, n = NT - 1 - j, hp * NT + j
            for half in range(2):
                kts = slice(half * HALF, (half + 1) * HALF)
                pool.wait_ge(u_hi_set, 2 * n + half + 1)
                pool.tensor_tensor(u_lo[:, kts, :], u_t[:, t, kts, :], u_hi[:, kts, :].bitcast(F32), ALU.subtract)\
                    .then_inc(u_lo_set, 1)

        def pe_project(pe, hp, j):
            n = hp * NT + j
            pe.wait_ge(qk_normed, n)
            pe.wait_ge(v_lo_set, n)
            if j == 0:
                pe.wait_ge(w_lo_set, hp * 4 + 4)
            for kt in range(KT):
                if kt % HALF == 0:
                    pe.wait_ge(u_lo_set, 2 * n + kt // HALF + 1)
                for a, w in ((u_hi, w_hi), (u_hi, w_lo), (u_lo, w_hi)):
                    last = pe.matmul(proj[:, 0:3 * HD], a[:, kt, :], w[:, kt, :],
                                     start=(kt == 0 and a is u_hi and w is w_hi),
                                     stop=(kt == KT - 1 and a is u_lo))
                if kt % HALF == HALF - 1:
                    last.then_inc(proj_half, 1)

        def act_square_qk(act, hp, j):
            n = hp * NT + j
            act.wait_ge(proj_half, 2 * n + 2)
            act.wait_ge(qk_summed, n)
            act.activation(qk_sq[:, :], proj[:, 0:2 * HD], ACT.Square, scale=DH ** -0.5).then_inc(qk_squared, 1)

        def act_v(act, hp, j):
            t, n = NT - 1 - j, hp * NT + j
            act.wait_ge(proj_half, 2 * n + 2)
            if not (isinstance(hp, int) and hp == 0):
                act.wait_ge(pv_done, (hp - 1) * GROUPS + groups_before(j + 1))
            act.activation(v_s[:, t, 0:HD], proj[:, 2 * HD:3 * HD], ACT.Copy).then_inc(v_hi_set, 1)

        def dve_v(dve, hp, j):
            t, n = NT - 1 - j, hp * NT + j
            dve.wait_ge(v_hi_set, n + 1)
            dve.tensor_tensor(v_s[:, t, HD:2 * HD], proj[:, 2 * HD:3 * HD], v_s[:, t, 0:HD].bitcast(F32),
                              ALU.subtract).then_inc(v_lo_set, 1)

        def dve_sum_qk(dve, hp, j):
            n = hp * NT + j
            dve.wait_ge(qk_squared, n + 1)
            dve.wait_ge(qk_var_set, n)
            dve.tensor_reduce(qk_ss[:, :], qk_sq[:, :].rearrange("p (g d) -> p g d", g=4), AX.X, ALU.add)\
               .then_inc(qk_summed, 1)

        def pool_project(pool, hp, j):
            n = hp * NT + j
            pool.wait_ge(qk_summed, n + 1)
            pool.wait_ge(qk_rs_set, n)
            pool.tensor_tensor(qk_var[:, :], qk_ss[:, :], eps[:, :], ALU.add).then_inc(qk_var_set, 1)
            pool.wait_ge(qk_var_set, n + 1)
            pool.wait_ge(qk_normed, n)
            pool.tensor_tensor(qk_rs[:, :], qk_var[:, :], minus_half[:, :], ALU.pow).then_inc(qk_rs_set, 1)

        def dve_norm_qk(dve, hp, j):
            n = hp * NT + j
            dve.wait_ge(qk_rs_set, n + 1)
            dve.wait_ge(qk_turned, n)
            dve.tensor_tensor(
                qk_nat[:, :, :, :],
                proj[:, 0:2 * HD].rearrange("p (g d) -> p g d", g=4).unsqueeze(2).to_broadcast([P, 4, 2, DH]),
                qk_rs[:, :].unsqueeze(2).unsqueeze(3).to_broadcast([P, 4, 2, DH]),
                ALU.mult).then_inc(qk_normed, 1)

        def pe_turn_qk(pe, hp, j, slot):
            n = hp * NT + j
            pe.wait_ge(qk_normed, n + 1)
            for g in range(4):
                last = pe.transpose(turn[:, slot, g * P:(g + 1) * P],
                                    qk_nat[:, g, :, :].rearrange("p a d -> p (a d)"), ident[:, :])
            last.then_inc(qk_turned, 1)

        def turned(slot, g, rows=slice(0, P)):
            return turn[rows, slot, g * 2 * P:(g + 1) * 2 * P].rearrange("p (m r) -> p m r", m=2)

        def act_turned_qk(act, hp, j, slot):
            t, n = NT - 1 - j, hp * NT + j
            rows = slice(t * P, (t + 1) * P)
            act.wait_ge(qk_turned, n + 1)
            if not (isinstance(hp, int) and hp == 0):
                act.wait_ge(scored, (hp - 1) * SCORED + 2 * groups_before(j + 1))
            act.activation(q_s[:, :, rows], turned(slot, 0), ACT.Copy, scale=g_q[:, :]).then_inc(q_hi_set, 1)
            act.activation(k_hi[:, :, rows], turned(slot, 1), ACT.Copy, scale=g_k[:, :]).then_inc(k_hi_set, 1)

        def dve_turned_qk(dve, hp, j, slot):
            t, n = NT - 1 - j, hp * NT + j
            rows, low = slice(t * P, (t + 1) * P), slice(DH, P)
            dve.wait_ge(k_hi_set, n + 1)
            dve.scalar_tensor_tensor(q_s[low, :, rows], turned(slot, 0, low), g_q[low, :],
                                     q_s[low, :, rows].bitcast(F32), ALU.mult, ALU.subtract)\
               .then_inc(q_lo_set, 1)
            dve.scalar_tensor_tensor(k_lo[:, :, rows], turned(slot, 1), g_k[:, :],
                                     k_hi[:, :, rows].bitcast(F32), ALU.mult, ALU.subtract)\
               .then_inc(k_lo_set, 1)

        with nc.Block() as block:
            @block.sync
            def _(sp):
                with nc.allow_non_contiguous_dma("gains and lambdas, once"):
                    for half in range(2):
                        sp.dma_start(g_q[half * DH:(half + 1) * DH, :], q_g.rearrange("a d -> d a"))\
                          .then_inc(consts_loaded, 16)
                        sp.dma_start(g_k[half * DH:(half + 1) * DH, :], k_g.rearrange("a d -> d a"))\
                          .then_inc(consts_loaded, 16)
                    sp.dma_start(g1_row, norm1_g.to_broadcast([P, D])).then_inc(consts_loaded, 16)
                    for n, v in enumerate(lambdas):
                        sp.dma_start(lam_v[:, n, :], v.to_broadcast([P, DH])).then_inc(consts_loaded, 16)
                for j in range(2):
                    sp.dma_start(x_in[:, j, :], x[(NT - 1 - j) * P:(NT - j) * P, :]).then_inc(x_loaded[j], 16)
                load_weights(sp, 0)
                for j in range(2, NT):
                    sp.wait_ge(u_normed, j - 1)
                    sp.dma_start(x_in[:, j % 2, :], x[(NT - 1 - j) * P:(NT - j) * P, :])\
                      .then_inc(x_loaded[j % 2], 16)

            @block.gpsimd
            def _(pool):
                pool.memset(ident[:, :], 0.0).then_inc(ident_set, 1)
                pool.wait_ge(ident_set, 1)
                pool.affine_select(out=ident[:, :], in_=ident[:, :], compare_op=ALU.not_equal, fill=1.0,
                                   base=0, pattern=[[-1, P]], channel_multiplier=1).then_inc(ident_set, 1)
                pool.memset(minus_half[:, :], -0.5).then_inc(ident_set, 1)
                pool.memset(eps[:, :], EPS).then_inc(ident_set, 1)

                def x_factor(j):
                    pool.wait_ge(x_squared, j + 1)
                    pool.tensor_tensor(x_var[:, j % 2:j % 2 + 1], x_ss[:, j % 2:j % 2 + 1], eps[:, 0:1], ALU.add)\
                        .then_inc(x_var_set, 1)
                    pool.wait_ge(x_var_set, j + 1)
                    if j >= 2:
                        pool.wait_ge(u_normed, j - 1)
                    pool.tensor_tensor(x_rs[:, j % 2:j % 2 + 1], x_var[:, j % 2:j % 2 + 1],
                                       minus_half[:, 0:1], ALU.pow).then_inc(x_rs_set, 1)

                pool.wait_ge(ident_set, 4)
                x_factor(0)
                x_factor(1)
                pool_split_weights(pool, 0)
                pool_split_u(pool, 0, 0)
                for j in range(NT):
                    if j + 2 < NT:
                        x_factor(j + 2)
                    if j + 1 < NT:
                        pool_split_u(pool, 0, j + 1)
                    pool_project(pool, 0, j)

            @block.scalar
            def _(act):
                def x_square(j):
                    act.wait_ge(x_loaded[j % 2], 16 * (j // 2 + 1))
                    if j >= 1:
                        act.wait_ge(x_squared, j)
                    if j >= 2:
                        act.wait_ge(x_var_set, j - 1)
                    act.activation(x_junk, x_in[:, j % 2, :], ACT.Square, scale=D ** -0.5,
                                   accum_out=x_ss[:, j % 2:j % 2 + 1]).then_inc(x_squared, 1)

                x_square(0)
                x_square(1)
                act.wait_ge(lam_step, 1)
                act.activation(lam_e[:, :], lam_s[:, :], ACT.Exp).then_inc(lam_step, 1)
                act_split_weights(act, 0)
                act.wait_ge(u_kept, 1)
                act_split_u(act, 0, 0)
                for j in range(NT):
                    if j + 2 < NT:
                        x_square(j + 2)
                    if j + 1 < NT:
                        act.wait_ge(u_kept, j + 2)
                        act_split_u(act, 0, j + 1, [0])
                    if j:
                        act_turned_qk(act, 0, j - 1, (j - 1) % 2)
                    if j + 1 < NT:
                        act_split_u(act, 0, j + 1, [1])
                    act_square_qk(act, 0, j)
                    act_v(act, 0, j)
                act_turned_qk(act, 0, NT - 1, (NT - 1) % 2)

            @block.vector
            def _(dve):
                def u_norm(j):
                    dve.wait_ge(x_rs_set, j + 1)
                    if j >= 2:
                        dve.wait_ge(u_turned, j - 1)
                    dve.scalar_tensor_tensor(u_nat[:, j % 2, :], x_in[:, j % 2, :], x_rs[:, j % 2:j % 2 + 1],
                                             g1_row, ALU.mult, ALU.mult).then_inc(u_normed, 1)

                def u_keep(j):
                    dve.wait_ge(u_turned, j + 1)
                    dve.tensor_copy(u_t[:, NT - 1 - j, :, :].rearrange("p a b -> p (a b)"),
                                    scores[:, 2 * (j % 2):2 * (j % 2) + 2, :].rearrange("p a b -> p (a b)"))\
                       .then_inc(u_kept, 1)

                for par in range(2):
                    dve.memset(o_n[:, par, :], 0.0).then_inc(o_stored[par], 16)
                dve.memset(mask_l[:, :], 0.0).then_inc(consts_set, 1)
                dve.memset(mask_r[:, :], 0.0).then_inc(consts_set, 1)
                dve.wait_ge(consts_set, 2)
                dve.memset(mask_l[0:1, 0:DH], 1.0).then_inc(consts_set, 1)
                dve.memset(mask_r[0:1, :], MASKED).then_inc(consts_set, 1)
                dve.wait_ge(consts_loaded, 16 * 9)
                dve.tensor_tensor(lam_w[:, :, :], lam_v[:, 0::2, :], lam_v[:, 1::2, :], ALU.mult)\
                   .then_inc(consts_set, 1)
                dve.wait_ge(consts_set, 5)
                dve.tensor_reduce(lam_s[:, :], lam_w[:, :, :], AX.X, ALU.add).then_inc(lam_step, 1)
                dve.wait_ge(lam_step, 2)
                dve.tensor_tensor(lam_d[:, :], lam_e[:, 1:2], lam_e[:, 0:1], ALU.subtract).then_inc(lam_step, 1)
                dve.wait_ge(lam_step, 3)
                dve.tensor_scalar(neg_lam[:, :], lam_d[:, :], LAMBDA_INIT, None, ALU.subtract)\
                   .then_inc(lam_step, 1)
                u_norm(0)
                u_norm(1)
                u_keep(0)
                for j in range(NT):
                    if j + 1 < NT:
                        u_keep(j + 1)
                    if j + 2 < NT:
                        u_norm(j + 2)
                    if j:
                        dve_turned_qk(dve, 0, j - 1, (j - 1) % 2)
                    dve_sum_qk(dve, 0, j)
                    dve_v(dve, 0, j)
                    dve_norm_qk(dve, 0, j)
                dve_turned_qk(dve, 0, NT - 1, (NT - 1) % 2)

            @block.tensor
            def _(pe):
                def turn_u(j):
                    pe.wait_ge(u_normed, j + 1)
                    if j >= 2:
                        pe.wait_ge(u_kept, j - 1)
                    for kt in range(KT):
                        last = pe.transpose(scores[:, 2 * (j % 2) + kt // TPB, (kt % TPB) * P:(kt % TPB + 1) * P],
                                            u_nat[:, j % 2, kt * P:(kt + 1) * P], ident[:, :])
                    last.then_inc(u_turned, 1)

                def turn_qk(j):
                    if j >= 2:
                        pe.wait_ge(k_lo_set, j - 1)
                    pe_turn_qk(pe, 0, j, j % 2)

                pe.wait_ge(ident_set, 4)
                turn_u(0)
                for j in range(NT):
                    if j + 1 < NT:
                        turn_u(j + 1)
                    pe_project(pe, 0, j)
                    if j:
                        turn_qk(j - 1)
                turn_qk(NT - 1)

        fills = {True: turn_order(True), False: turn_order(False)}
        assert len(fills[True]) % 2 == 0 and NT % 2 == 0

        def slot_of(what, projecting):
            return fills[projecting].index(what) % 2

        def wait_slot(pe, h, what, projecting):
            at = fills[projecting].index(what)
            if at < 2:
                return
            last = fills[projecting][at - 2]
            if last[0] == "p":
                pe.wait_ge(pt_lo_set, h * GROUPS + groups_before(last[1]) + last[2] + 1)
            else:
                pe.wait_ge(k_lo_set, (h + 1) * NT + last[1] + 1)

        def pe_scores(pe, h, j, m):
            t = NT - 1 - j
            for n, bank in enumerate(bank_order(j)):
                if m == 1:
                    pe.wait_ge(exp_done, h * SCORED + score_index(j, 0, n) + 1)
                elif j:
                    before = bank_order(j - 1).index(bank)
                    pe.wait_ge(exp_done, h * SCORED + score_index(j - 1, 1, before) + 1)
                else:
                    pe.wait_ge(k_lo_set, h * NT + NT - TPB * bank)
                width = bank_width(j, bank)
                q = q_s[:, m, t * P:(t + 1) * P]
                keys = slice(bank * BANK, bank * BANK + width)
                masked = bank == banks_of(j) - 1
                if masked:
                    pe.matmul(scores[:, bank, width - DH:width], mask_l[:, :], mask_r[:, :],
                              start=True, stop=False, skip_group_check=True)
                pe.matmul(scores[:, bank, 0:width], q, k_hi[:, m, keys], start=not masked, stop=False,
                          skip_group_check=True)
                last = pe.matmul(scores[:, bank, 0:width], q, k_lo[:, m, keys], start=False, stop=True,
                                 skip_group_check=True)
                last.then_inc(scored, 1)

        def dve_max(dve, h, j, m):
            par, nb = j % 2, banks_of(j)
            for n, bank in enumerate(bank_order(j)):
                dve.wait_ge(scored, h * SCORED + score_index(j, m, n) + 1)
                dve.tensor_reduce(mx[:, par, m, n:n + 1], scores[:, bank, 0:bank_width(j, bank)], AX.X, ALU.max)\
                   .then_inc(bank_max, 1)
            dve.wait_ge(bank_max, h * SCORED + score_index(j, m, nb))
            dve.tensor_reduce(m_all[:, par, m:m + 1], mx[:, par, m, 0:nb], AX.X, ALU.max).then_inc(row_max, 1)
            dve.wait_ge(row_max, h * 2 * NT + 2 * j + m + 1)
            dve.tensor_scalar(nbias[:, par, m:m + 1], m_all[:, par, m:m + 1], -SCALE, None, ALU.mult)\
               .then_inc(bias_set, 1)

        def act_exps(act, h, j, m):
            par = j % 2
            act.wait_ge(bias_set, h * 2 * NT + 2 * j + m + 1)
            if m == 0 and j >= 2:
                act.wait_ge(p_turned, h * GROUPS + groups_before(j - 1))
            if m == 1 and j:
                act.wait_ge(combined, h * GROUPS + groups_before(j))
            for n, bank in enumerate(bank_order(j)):
                width = bank_width(j, bank)
                dst = (p_all[:, par, :] if m == 0 else p1)[:, bank * BANK:bank * BANK + width]
                act.activation(dst, scores[:, bank, 0:width], ACT.Exp, bias=nbias[:, par, m:m + 1], scale=SCALE,
                               accum_out=z_part[:, par, m, n:n + 1]).then_inc(exp_done, 1)

        def dve_combine(dve, h, j):
            par, nb = j % 2, banks_of(j)
            dve.wait_ge(exp_done, h * SCORED + 2 * groups_before(j + 1))
            dve.tensor_reduce(z[:, par, :], z_part[:, par, :, 0:nb], AX.X, ALU.add).then_inc(z_summed, 1)
            dve.wait_ge(z_summed, h * NT + j + 1)
            dve.reciprocal(rz[:, par, :], z[:, par, :]).then_inc(z_inverted, 1)
            dve.wait_ge(z_inverted, h * NT + j + 1)
            dve.tensor_scalar(neg_c[:, par:par + 1], z[:, par, 0:1], rz[:, par, 1:2], neg_lam[:, :],
                              ALU.mult, ALU.mult).then_inc(c_set, 1)
            dve.wait_ge(c_set, h * NT + j + 1)
            for bank in bank_order(j):
                cols = slice(bank * BANK, bank * BANK + bank_width(j, bank))
                dve.scalar_tensor_tensor(p_all[:, par, cols], p1[:, cols], neg_c[:, par:par + 1],
                                         p_all[:, par, cols], ALU.mult, ALU.add).then_inc(combined, 1)

        def pe_turn_p(pe, h, j, n, projecting):
            bank = bank_order(j)[n]
            pe.wait_ge(combined, h * GROUPS + groups_before(j) + n + 1)
            wait_slot(pe, h, ("p", j, n), projecting)
            slot = slot_of(("p", j, n), projecting)
            for c in range(bank_width(j, bank) // P):
                at = bank * BANK + c * P
                last = pe.transpose(turn[:, slot, c * P:(c + 1) * P], p_all[:, j % 2, at:at + P], ident[:, :])
            last.then_inc(p_turned, 1)

        def act_turned_p(act, h, j, n, projecting):
            g = groups_before(j) + n
            width = bank_width(j, bank_order(j)[n])
            act.wait_ge(p_turned, h * GROUPS + g + 1)
            if g >= 2:
                act.wait_ge(pv_done, h * GROUPS + g - 1)
            act.activation(pt_hi[:, g % 2, 0:width], turn[:, slot_of(("p", j, n), projecting), 0:width], ACT.Copy)\
               .then_inc(pt_hi_set, 1)

        def dve_turned_p(dve, h, j, n, projecting):
            g = groups_before(j) + n
            width = bank_width(j, bank_order(j)[n])
            dve.wait_ge(pt_hi_set, h * GROUPS + g + 1)
            dve.tensor_tensor(pt_lo[:, g % 2, 0:width], turn[:, slot_of(("p", j, n), projecting), 0:width],
                              pt_hi[:, g % 2, 0:width].bitcast(F32), ALU.subtract).then_inc(pt_lo_set, 1)

        def pe_values(pe, h, j, n):
            g, bank, nb = groups_before(j) + n, bank_order(j)[n], banks_of(j)
            tiles = bank_width(j, bank) // P
            if n == 0 and j:
                pe.wait_ge(o_summed, h * NT + j)
            if j == 0:
                pe.wait_ge(v_lo_set, h * NT + NT - TPB * bank)
            pe.wait_ge(pt_lo_set, h * GROUPS + g + 1)
            for c in range(tiles):
                v = v_s[:, bank * TPB + c, :]
                pe.matmul(o_acc[:, 0:2 * HD], pt_hi[:, g % 2, c * P:(c + 1) * P], v, start=(n == 0 and c == 0),
                          stop=False, skip_group_check=True)
                last = pe.matmul(o_acc[:, 0:HD], pt_lo[:, g % 2, c * P:(c + 1) * P], v[:, 0:HD], start=False,
                                 stop=(n == nb - 1 and c == tiles - 1), skip_group_check=True)
            last.then_inc(pv_done, 1)

        def act_output_low(act, h, j):
            par, a = j % 2, h * NT + j
            act.wait_ge(pv_done, h * GROUPS + groups_before(j + 1))
            act.wait_ge(z_inverted, a + 1)
            act.activation(o_tmp[:, par, :], o_acc[:, HD:2 * HD], ACT.Copy, scale=rz[:, par, 0:1])\
               .then_inc(o_low_set, 1)

        def act_square_output(act, h, j):
            par, a = j % 2, h * NT + j
            act.wait_ge(o_summed, a + 1)
            act.activation(o_sq[:, :], o_sum[:, par, :], ACT.Square, scale=HD ** -0.5,
                           accum_out=o_ss[:, par:par + 1])\
               .then_inc(o_squared, 1)

        def dve_output(dve, h, j):
            par, a = j % 2, h * NT + j
            dve.wait_ge(o_low_set, a + 1)
            if j >= 2:
                dve.wait_ge(o_normed, h * NT + j - 1)
            dve.scalar_tensor_tensor(o_sum[:, par, :], o_acc[:, 0:HD], rz[:, par, 0:1], o_tmp[:, par, :],
                                     ALU.mult, ALU.add).then_inc(o_summed, 1)

        def pool_output(pool, h, j):
            par, a = j % 2, h * NT + j
            pool.wait_ge(o_squared, a + 1)
            pool.tensor_tensor(o_var[:, par:par + 1], o_ss[:, par:par + 1], eps[:, 0:1], ALU.add)\
                .then_inc(o_var_set, 1)
            pool.wait_ge(o_var_set, a + 1)
            pool.tensor_tensor(o_rs[:, par:par + 1], o_var[:, par:par + 1], minus_half[:, 0:1], ALU.pow)\
                .then_inc(o_rs_set, 1)

        def act_norm_output(act, h, j):
            par, a = j % 2, h * NT + j
            act.wait_ge(o_rs_set, a + 1)
            act.wait_ge(o_stored[par], 16 * (h * (NT // 2) + j // 2 + 1))
            act.activation(o_n[:, par, :], o_sum[:, par, :], ACT.Copy, scale=o_rs[:, par:par + 1])\
               .then_inc(o_normed, 1)

        def sp_head(sp, h, projecting):
            cols = bass.ds(h * HD, HD)
            if projecting:
                load_weights(sp, h + 1)
            for j in range(NT):
                t = NT - 1 - j
                sp.wait_ge(o_normed, h * NT + j + 1)
                sp.dma_start(o_dram[t * P:(t + 1) * P, cols], o_n[:, j % 2, :])\
                  .then_inc(o_stored[j % 2], 16)

        def pe_head(pe, h, projecting):
            for j in range(NT + 1):
                nb = banks_of(j - 1) if j else 0
                if j < NT:
                    pe_scores(pe, h, j, 0)
                if projecting and j:
                    pe_project(pe, h + 1, j - 1)
                for n in range(min(nb, 2)):
                    pe_turn_p(pe, h, j - 1, n, projecting)
                if j < NT:
                    pe_scores(pe, h, j, 1)
                for n in range(2, nb):
                    pe_values(pe, h, j - 1, n - 2)
                    pe_turn_p(pe, h, j - 1, n, projecting)
                if nb > 1:
                    pe_values(pe, h, j - 1, nb - 2)
                if projecting and j:
                    wait_slot(pe, h, ("qk", j - 1), True)
                    pe_turn_qk(pe, h + 1, j - 1, slot_of(("qk", j - 1), True))
                if nb:
                    pe_values(pe, h, j - 1, nb - 1)

        def act_head(act, h, projecting):
            def finish(j):
                if projecting:
                    act_v(act, h + 1, j)
                act_output_low(act, h, j)
                if projecting:
                    act_turned_qk(act, h + 1, j, slot_of(("qk", j), True))

            for j in range(NT + 1):
                nb = banks_of(j - 1) if j else 0
                if j >= 2:
                    finish(j - 2)
                if j < NT:
                    act_exps(act, h, j, 0)
                if projecting and j == 0:
                    act_split_weights(act, h + 1)
                if j >= 2:
                    act_square_output(act, h, j - 2)
                if projecting and j:
                    act_square_qk(act, h + 1, j - 1)
                for n in range(min(nb, 2)):
                    act_turned_p(act, h, j - 1, n, projecting)
                if j >= 2:
                    act_norm_output(act, h, j - 2)
                if projecting and j < NT:
                    act_split_u(act, h + 1, j)
                for n in range(2, nb):
                    act_turned_p(act, h, j - 1, n, projecting)
                if j < NT:
                    act_exps(act, h, j, 1)
            finish(NT - 1)
            act_square_output(act, h, NT - 1)
            act_norm_output(act, h, NT - 1)

        def dve_head(dve, h, projecting):
            def finish(j):
                if projecting:
                    dve_v(dve, h + 1, j)
                dve_output(dve, h, j)

            for j in range(NT + 1):
                nb = banks_of(j - 1) if j else 0
                if j >= 2:
                    finish(j - 2)
                if j < NT:
                    dve_max(dve, h, j, 0)
                if j:
                    dve_combine(dve, h, j - 1)
                if projecting and j >= 2:
                    dve_turned_qk(dve, h + 1, j - 2, slot_of(("qk", j - 2), True))
                if projecting and j:
                    dve_sum_qk(dve, h + 1, j - 1)
                for n in range(min(nb, 2)):
                    dve_turned_p(dve, h, j - 1, n, projecting)
                if j < NT:
                    dve_max(dve, h, j, 1)
                for n in range(2, nb):
                    if n == nb - 1 and projecting:
                        dve_norm_qk(dve, h + 1, j - 1)
                    dve_turned_p(dve, h, j - 1, n, projecting)
                if projecting and j and nb <= 2:
                    dve_norm_qk(dve, h + 1, j - 1)
            finish(NT - 1)
            if projecting:
                dve_turned_qk(dve, h + 1, NT - 1, slot_of(("qk", NT - 1), True))

        def pool_head(pool, h, projecting):
            if projecting:
                pool_split_weights(pool, h + 1)
            for j in range(NT + 1):
                if j >= 2:
                    pool_output(pool, h, j - 2)
                if projecting and j:
                    pool_project(pool, h + 1, j - 1)
                if projecting and j < NT:
                    pool_split_u(pool, h + 1, j)
            pool_output(pool, h, NT - 1)

        with nc.Block() as block:
            @block.sync
            def _(sp):
                with sp.Fori(0, H - 1) as h:
                    sp_head(sp, h, True)
                sp_head(sp, H - 1, False)
                for par in range(2):
                    sp.wait_ge(o_stored[par], 16 * (H * NT // 2 + 1))

            @block.gpsimd
            def _(pool):
                with pool.Fori(0, H - 1) as h:
                    pool_head(pool, h, True)
                pool_head(pool, H - 1, False)

            @block.scalar
            def _(act):
                with act.Fori(0, H - 1) as h:
                    act_head(act, h, True)
                act_head(act, H - 1, False)

            @block.vector
            def _(dve):
                with dve.Fori(0, H - 1) as h:
                    dve_head(dve, h, True)
                dve_head(dve, H - 1, False)

            @block.tensor
            def _(pe):
                with pe.Fori(0, H - 1) as h:
                    pe_head(pe, h, True)
                pe_head(pe, H - 1, False)


def output_step(nc, x, o_dram, w_out, sub_g, norm2_g, h_dram, u2_dram):
    with ExitStack() as ctx:
        def sb(name, shape, dt=F32):
            return ctx.enter_context(nc.sbuf_tensor(name, shape, dt))

        def sem(name):
            return ctx.enter_context(nc.semaphore(name))

        RAW = 3
        w_raw = sb("wo_raw", [P, RAW, D])
        w_hi = sb("wo_hi", [P, KT, D], F32R)
        w_lo = sb("wo_lo", [P, KT, D], F32R)
        o_in = sb("o_in", [P, 2, D])
        x_in = sb("x_res", [P, 2, D])
        ot_hi = sb("ot_hi", [P, 2, D], F32R)
        ot_lo = sb("ot_lo", [P, 2, D], F32R)
        h_out = sb("h_out", [P, 2, D])
        h_sq = sb("h_sq", [P, D])
        h_ss = sb("h_ss", [P, 2])
        h_var = sb("h_var", [P, 2])
        h_rs = sb("h_rs", [P, 2])
        u_nat = sb("u2_nat", [P, 2, D])
        u_hi = sb("u2_hi_tile", [P, 2, D], F32R)
        u_lo = sb("u2_lo_tile", [P, 2, D], F32R)
        ident = sb("ident3", [P, P])
        minus_half = sb("minus_half3", [P, 1])
        eps = sb("eps3", [P, 1])
        g_raw = sb("sub_g_raw", [P, 1])
        g_o = sb("sub_g_col", [P, 1])
        g2_row = sb("g2_row", [P, D])
        o_turn = ctx.enter_context(nc.psum_tensor("o_turn", [P, D], F32))
        u_turn = ctx.enter_context(nc.psum_tensor("u_turn", [P, D], F32))
        product = ctx.enter_context(nc.psum_tensor("product", [P, 2, D], F32))

        gain_loaded, g2_loaded, ident_set, g_set = (
            sem("gain_loaded"), sem("g2_loaded"), sem("ident3_set"), sem("g3_set"))
        w_loaded = [sem(f"wo_loaded{n}") for n in range(RAW)]
        w_hi_set, w_lo_set = sem("wo_hi_set"), sem("wo_lo_set")
        o_loaded = [sem("o_loaded0"), sem("o_loaded1")]
        x_loaded = [sem("xr_loaded0"), sem("xr_loaded1")]
        o_turned, ot_hi_set, ot_lo_set = sem("o_turned"), sem("ot_hi_set"), sem("ot_lo_set")
        multiplied, h_set, h_squared = sem("multiplied"), sem("h_set"), sem("h_squared")
        h_var_set, h_rs_set, u_normed, u_turned = (
            sem("h_var_set"), sem("h_rs_set"), sem("u2_normed"), sem("u2_turned"))
        u_hi_set, u_lo_set = sem("u2_hi_set"), sem("u2_lo_set")
        h_stored = [sem("h_stored0"), sem("h_stored1")]
        u_stored = [sem("u2_stored0"), sem("u2_stored1")]

        LAST = NT // 2 - 1

        def rounds(engine, tile):
            for r in range(2):
                for q in range(2):
                    tile(r, q)
            with engine.Fori(2, LAST) as r:
                for q in range(2):
                    tile(r, q)
            for q in range(2):
                tile(LAST, q)

        def static(r, value):
            return isinstance(r, int) and r == value

        def before(r, q):
            return (r, 0) if q else (r - 1, 1)

        def after(r, q):
            return (r + 1, 0) if q else (r, 1)

        with nc.Block() as block:
            @block.sync
            def _(sp):
                def rows(r, q):
                    row = (r * 2 + q) * P
                    return bass.ds(row if isinstance(row, int) else sp.snap(row), P)

                def load(r, q, at):
                    if not static(r, 0):
                        sp.wait_ge(o_turned, r * 2 + q - 1)
                    sp.dma_start(o_in[:, q, :], o_dram[at, :]).then_inc(o_loaded[q], 16)
                    sp.dma_start(x_in[:, q, :], x[at, :]).then_inc(x_loaded[q], 16)

                def store_u(r, q, at):
                    sp.wait_ge(u_lo_set, r * 2 + q + 1)
                    sp.dma_start(u2_dram[0, at, :], u_hi[:, q, :].bitcast(F32)).then_inc(u_stored[q], 16)
                    sp.dma_start(u2_dram[1, at, :], u_lo[:, q, :].bitcast(F32)).then_inc(u_stored[q], 16)

                def tile(r, q):
                    ats = {"last": rows(*before(r, q)), "this": rows(r, q), "next": rows(r + 1, q)}
                    if not (static(r, 0) and q == 0):
                        store_u(*before(r, q), ats["last"])
                    sp.wait_ge(h_set, r * 2 + q + 1)
                    sp.dma_start(h_dram[ats["this"], :], h_out[:, q, :]).then_inc(h_stored[q], 16)
                    if not static(r, LAST):
                        load(r + 1, q, ats["next"])

                with nc.allow_non_contiguous_dma("a gain, once"):
                    sp.dma_start(g_raw[:, :], sub_g.rearrange("a d -> d a")).then_inc(gain_loaded, 16)
                load(0, 0, rows(0, 0))
                load(0, 1, rows(0, 1))
                for kt in range(KT):
                    if kt >= RAW:
                        sp.wait_ge(w_lo_set, kt - RAW + 1)
                    sp.dma_start(w_raw[:, kt % RAW, :], w_out[kt * P:(kt + 1) * P, :])\
                      .then_inc(w_loaded[kt % RAW], 16)
                sp.dma_start(g2_row[:, :], norm2_g.to_broadcast([P, D])).then_inc(g2_loaded, 16)
                rounds(sp, tile)
                store_u(LAST, 1, rows(LAST, 1))
                for q in range(2):
                    sp.wait_ge(h_stored[q], 16 * NT // 2)
                    sp.wait_ge(u_stored[q], 32 * NT // 2)

            @block.gpsimd
            def _(pool):
                pool.memset(ident[:, :], 0.0).then_inc(ident_set, 1)
                pool.wait_ge(ident_set, 1)
                pool.affine_select(out=ident[:, :], in_=ident[:, :], compare_op=ALU.not_equal, fill=1.0,
                                   base=0, pattern=[[-1, P]], channel_multiplier=1).then_inc(ident_set, 1)
                pool.memset(minus_half[:, :], -0.5).then_inc(ident_set, 1)
                pool.memset(eps[:, :], EPS).then_inc(ident_set, 1)
                pool.wait_ge(ident_set, 4)

                def tile(r, q):
                    n = r * 2 + q
                    pool.wait_ge(h_squared, n + 1)
                    pool.tensor_tensor(h_var[:, q:q + 1], h_ss[:, q:q + 1], eps[:, :], ALU.add)\
                        .then_inc(h_var_set, 1)
                    pool.wait_ge(h_var_set, n + 1)
                    pool.tensor_tensor(h_rs[:, q:q + 1], h_var[:, q:q + 1], minus_half[:, :], ALU.pow)\
                        .then_inc(h_rs_set, 1)

                rounds(pool, tile)

            @block.scalar
            def _(act):
                def split_o(r, q):
                    n = r * 2 + q
                    act.wait_ge(o_turned, n + 1)
                    if not static(r, 0):
                        act.wait_ge(multiplied, 2 * (n - 1))
                    act.activation(ot_hi[:, q, :], o_turn[:, :], ACT.Copy, scale=g_o[:, :]).then_inc(ot_hi_set, 1)

                def split_u(r, q):
                    act.wait_ge(u_turned, r * 2 + q + 1)
                    act.wait_ge(u_stored[q], 32 * r)
                    act.activation(u_hi[:, q, :], u_turn[:, :], ACT.Copy).then_inc(u_hi_set, 1)

                def tile(r, q):
                    n = r * 2 + q
                    if not (static(r, 0) and q == 0):
                        split_u(*before(r, q))
                    if not (static(r, LAST) and q == 1):
                        split_o(*after(r, q))
                    act.wait_ge(h_set, n + 1)
                    act.wait_ge(h_squared, n)
                    if not static(r, 0):
                        act.wait_ge(h_var_set, n - 1)
                    act.activation(h_sq[:, :], h_out[:, q, :], ACT.Square, scale=D ** -0.5,
                                   accum_out=h_ss[:, q:q + 1])\
                       .then_inc(h_squared, 1)

                act.wait_ge(gain_loaded, 16)
                act.activation(g_o[:, :], g_raw[:, :], ACT.Copy, scale=1.0 - LAMBDA_INIT).then_inc(g_set, 1)
                act.wait_ge(g_set, 1)
                split_o(0, 0)
                for kt in range(KT):
                    act.wait_ge(w_loaded[kt % RAW], 16 * (kt // RAW + 1))
                    act.activation(w_hi[:, kt, :], w_raw[:, kt % RAW, :], ACT.Copy).then_inc(w_hi_set, 1)
                rounds(act, tile)
                split_u(LAST, 1)

            @block.vector
            def _(dve):
                def split_o(r, q):
                    n = r * 2 + q
                    dve.wait_ge(ot_hi_set, n + 1)
                    dve.scalar_tensor_tensor(ot_lo[:, q, :], o_turn[:, :], g_o[:, :], ot_hi[:, q, :].bitcast(F32),
                                             ALU.mult, ALU.subtract).then_inc(ot_lo_set, 1)

                def norm_u(r, q):
                    n = r * 2 + q
                    dve.wait_ge(h_rs_set, n + 1)
                    if not static(r, 0):
                        dve.wait_ge(u_turned, n - 1)
                    dve.scalar_tensor_tensor(u_nat[:, q, :], h_out[:, q, :], h_rs[:, q:q + 1], g2_row[:, :],
                                             ALU.mult, ALU.mult).then_inc(u_normed, 1)

                def split_u(r, q):
                    dve.wait_ge(u_hi_set, r * 2 + q + 1)
                    dve.tensor_tensor(u_lo[:, q, :], u_turn[:, :], u_hi[:, q, :].bitcast(F32), ALU.subtract)\
                       .then_inc(u_lo_set, 1)

                def tile(r, q):
                    n = r * 2 + q
                    if not (static(r, 0) and q == 0):
                        norm_u(*before(r, q))
                        split_u(*before(r, q))
                    if not (static(r, LAST) and q == 1):
                        split_o(*after(r, q))
                    dve.wait_ge(multiplied, 2 * n + 2)
                    dve.wait_ge(x_loaded[q], 16 * (r + 1))
                    dve.wait_ge(h_stored[q], 16 * r)
                    if not static(r, 0):
                        dve.wait_ge(u_normed, n - 1)
                    dve.tensor_tensor(h_out[:, q, :], product[:, q, :], x_in[:, q, :], ALU.add).then_inc(h_set, 1)

                split_o(0, 0)
                for kt in range(KT):
                    dve.wait_ge(w_hi_set, kt + 1)
                    dve.tensor_tensor(w_lo[:, kt, :], w_raw[:, kt % RAW, :], w_hi[:, kt, :].bitcast(F32),
                                      ALU.subtract).then_inc(w_lo_set, 1)
                dve.wait_ge(g2_loaded, 16)
                rounds(dve, tile)
                norm_u(LAST, 1)
                split_u(LAST, 1)

            @block.tensor
            def _(pe):
                def turn_o(r, q):
                    n = r * 2 + q
                    pe.wait_ge(o_loaded[q], 16 * (r + 1))
                    pe.wait_ge(ot_lo_set, n)
                    for kt in range(KT):
                        last = pe.transpose(o_turn[:, kt * P:(kt + 1) * P], o_in[:, q, kt * P:(kt + 1) * P],
                                            ident[:, :])
                    last.then_inc(o_turned, 1)

                def turn_u(r, q):
                    n = r * 2 + q
                    pe.wait_ge(u_normed, n + 1)
                    pe.wait_ge(u_lo_set, n)
                    for kt in range(KT):
                        last = pe.transpose(u_turn[:, kt * P:(kt + 1) * P], u_nat[:, q, kt * P:(kt + 1) * P],
                                            ident[:, :])
                    last.then_inc(u_turned, 1)

                def half(r, q, dh):
                    cols = slice(dh * BANK, (dh + 1) * BANK)
                    if dh == 0:
                        pe.wait_ge(ot_lo_set, r * 2 + q + 1)
                        if not static(r, 0):
                            pe.wait_ge(h_set, r * 2 + q - 1)
                    for kt in range(KT):
                        if static(r, 0) and q == 0 and dh == 0:
                            pe.wait_ge(w_lo_set, kt + 1)
                        for a, w in ((ot_hi, w_hi), (ot_hi, w_lo), (ot_lo, w_hi)):
                            last = pe.matmul(product[:, q, cols], a[:, q, kt * P:(kt + 1) * P], w[:, kt, cols],
                                             start=(kt == 0 and a is ot_hi and w is w_hi),
                                             stop=(kt == KT - 1 and a is ot_lo))
                    last.then_inc(multiplied, 1)

                def tile(r, q):
                    half(r, q, 0)
                    if not (static(r, 0) and q == 0):
                        turn_u(*before(r, q))
                    if not (static(r, LAST) and q == 1):
                        turn_o(*after(r, q))
                    half(r, q, 1)

                pe.wait_ge(ident_set, 4)
                turn_o(0, 0)
                rounds(pe, tile)
                turn_u(LAST, 1)


def mlp_step(nc, h_dram, u2_dram, w1, w2, out):
    with ExitStack() as ctx:
        def sb(name, shape, dt=F32):
            return ctx.enter_context(nc.sbuf_tensor(name, shape, dt))

        def sem(name):
            return ctx.enter_context(nc.semaphore(name))

        CT = 8
        CHUNKS = NT // CT
        FT = 4
        NB = DFF // (FT * P)
        NH = CT * P // BANK
        E = FT * NH
        G = 2 * CT
        W1N, W2N = FT, 4

        u_hi = sb("u4_hi", [P, CT, KT, P], F32R)
        u_lo = sb("u4_lo", [P, CT, KT, P], F32R)
        y = sb("y", [P, CT, D])
        hid_hi = sb("hid_hi", [P, FT, CT * P], F32R)
        hid_lo = sb("hid_lo", [P, FT, CT * P], F32R)
        w1_raw = sb("w1_raw", [P, 2, KT, P])
        w1_hi = sb("w1_hi", [P, 2, KT, P], F32R)
        w1_lo = sb("w1_lo", [P, 2, KT, P], F32R)
        w2_raw = sb("w2_raw", [P, 2, 2, BANK])
        w2_hi = sb("w2_hi", [P, 2, FT, BANK], F32R)
        w2_lo = sb("w2_lo", [P, 2, FT, BANK], F32R)
        relu = sb("relu", [P, 2, BANK])
        relu_sq = sb("relu_sq", [P, 2, BANK])
        banks = ctx.enter_context(nc.psum_tensor("banks", [P, 8, BANK], F32))

        u_loaded = [sem(f"u4_loaded{n}") for n in range(NH)]
        y_loaded, y_stored = sem("y_loaded"), sem("y_stored")
        w1_loaded = [sem("w1_loaded0"), sem("w1_loaded1")]
        w2_loaded = [sem("w2_loaded0"), sem("w2_loaded1")]
        w1_hi_set, w1_lo_set, w2_hi_set, w2_lo_set = (
            sem("w1_hi_set"), sem("w1_lo_set"), sem("w2_hi_set"), sem("w2_lo_set"))
        hid_done, relu_set, sq_set, hid_hi_set, hid_lo_set = (
            sem("hid_done"), sem("relu_set"), sem("sq_set"), sem("hid_hi_set"), sem("hid_lo_set"))
        y_done, y_added = sem("y_done"), sem("y_added")

        w1_view = w1.rearrange("(kt p) f -> p kt f", p=P)
        w2_view = w2.rearrange("(ft p) d -> p ft d", p=P)
        u_view = u2_dram.rearrange("a (t p) d -> a p t d", p=P)
        h_view = h_dram.rearrange("(t p) d -> p t d", p=P)

        def blocks(engine, block):
            for c in range(CHUNKS):
                block(0, c * NB, c)
                with engine.Fori(1, NB) as b:
                    block(b, b + c * NB, None)

        def static(it, value):
            return isinstance(it, int) and it == value

        with nc.Block() as block:
            @block.sync
            def _(sp):
                def at(value):
                    return value if isinstance(value, int) else sp.snap(value)

                def loads(b, it, chunk):
                    w1_cols = [bass.ds(at(b * (FT * P) + n * P), P) for n in range(FT)]
                    w2_tiles = [bass.ds(at(b * FT + f), 2) for f in (0, 2)]
                    for n in range(FT):
                        if not (static(it, 0) and n < 2):
                            sp.wait_ge(w1_lo_set, it * W1N + n - 1)
                        sp.dma_start(w1_raw[:, n % 2, :, :], w1_view[:, :, w1_cols[n]])\
                          .then_inc(w1_loaded[n % 2], 16)
                        if not (static(it, 0) and n < 2):
                            sp.wait_ge(w2_lo_set, it * W2N + n - 1)
                        dh = n // 2
                        sp.dma_start(w2_raw[:, n % 2, :, :],
                                     w2_view[:, w2_tiles[n % 2], dh * BANK:(dh + 1) * BANK])\
                          .then_inc(w2_loaded[n % 2], 16)

                blocks(sp, loads)

            @block.gpsimd
            def _(pool):
                def split_w1(it, n):
                    pool.wait_ge(w1_hi_set, it * W1N + n + 1)
                    pool.tensor_tensor(w1_lo[:, n % 2, :, :], w1_raw[:, n % 2, :, :],
                                       w1_hi[:, n % 2, :, :].bitcast(F32), ALU.subtract).then_inc(w1_lo_set, 1)

                def body(b, it, chunk):
                    split_w1(it, 0)
                    split_w1(it, 1)
                    for j in range(FT):
                        for n in range(NH):
                            pool.wait_ge(hid_hi_set, it * E + j * NH + n + 1)
                            rows = slice(n * BANK, (n + 1) * BANK)
                            pool.tensor_tensor(hid_lo[:, j, rows], relu_sq[:, n, :],
                                               hid_hi[:, j, rows].bitcast(F32), ALU.subtract)\
                                .then_inc(hid_lo_set, 1)
                        if j + 2 < FT:
                            split_w1(it, j + 2)

                blocks(pool, body)

            @block.scalar
            def _(act):
                def load_u(c):
                    for n in range(NH):
                        tiles = slice(n * TPB, (n + 1) * TPB)
                        for a, u in enumerate((u_hi, u_lo)):
                            act.dma_start(u[:, tiles, :, :].rearrange("p t k r -> p t (k r)").bitcast(F32),
                                          u_view[a, :, c * CT + n * TPB:c * CT + (n + 1) * TPB, :])\
                               .then_inc(u_loaded[n], 16)

                def store_y(c):
                    for t in range(CT):
                        act.wait_ge(y_added, (c + 1) * NB * G - CT + t + 1)
                        row = (c * CT + t) * P
                        act.dma_start(out[row:row + P, :], y[:, t, :]).then_inc(y_stored, 16)

                def split_w1(it, n):
                    act.wait_ge(w1_loaded[n % 2], 16 * (it * 2 + n // 2 + 1))
                    if n >= 2:
                        act.wait_ge(hid_done, it * E + (n - 1) * NH)
                    else:
                        act.wait_ge(hid_done, it * E)
                    act.activation(w1_hi[:, n % 2, :, :], w1_raw[:, n % 2, :, :], ACT.Copy).then_inc(w1_hi_set, 1)

                def body(b, it, chunk):
                    if chunk is not None:
                        act.wait_ge(hid_done, it * E)
                        load_u(chunk)
                    split_w1(it, 0)
                    split_w1(it, 1)
                    if chunk is not None:
                        if chunk:
                            store_y(chunk - 1)
                            act.wait_ge(y_stored, 16 * CT * chunk)
                        act.dma_start(y[:, :, :], h_view[:, chunk * CT:(chunk + 1) * CT, :]).then_inc(y_loaded, 16)
                    for j in range(FT):
                        for n in range(NH):
                            e = it * E + j * NH + n
                            act.wait_ge(hid_done, e + 1)
                            act.activation(relu[:, n, :], banks[:, j * NH + n, :], ACT.Relu).then_inc(relu_set, 1)
                            act.wait_ge(sq_set, e + 1)
                            act.wait_ge(y_done, it * G)
                            act.activation(hid_hi[:, j, n * BANK:(n + 1) * BANK], relu_sq[:, n, :], ACT.Copy)\
                               .then_inc(hid_hi_set, 1)
                        if j + 2 < FT:
                            split_w1(it, j + 2)
                        act.wait_ge(w2_loaded[j % 2], 16 * (it * 2 + j // 2 + 1))
                        act.activation(w2_hi[:, j // 2, (j % 2) * 2:(j % 2) * 2 + 2, :], w2_raw[:, j % 2, :, :],
                                       ACT.Copy).then_inc(w2_hi_set, 1)

                blocks(act, body)
                store_y(CHUNKS - 1)
                act.wait_ge(y_stored, 16 * NT)

            @block.vector
            def _(dve):
                def body(b, it, chunk):
                    for j in range(FT):
                        for n in range(NH):
                            e = it * E + j * NH + n
                            dve.wait_ge(relu_set, e + 1)
                            if j * NH + n >= 2:
                                dve.wait_ge(hid_lo_set, e - 1)
                            else:
                                dve.wait_ge(hid_lo_set, it * E)
                            dve.scalar_tensor_tensor(relu_sq[:, n, :], banks[:, j * NH + n, :], 0.0, relu[:, n, :],
                                                     ALU.max, ALU.mult).then_inc(sq_set, 1)
                        dve.wait_ge(w2_hi_set, it * W2N + j + 1)
                        piece = (slice(None), j // 2, slice((j % 2) * 2, (j % 2) * 2 + 2))
                        dve.tensor_tensor(w2_lo[piece], w2_raw[:, j % 2, :, :], w2_hi[piece].bitcast(F32),
                                          ALU.subtract).then_inc(w2_lo_set, 1)
                    if chunk is not None:
                        dve.wait_ge(y_loaded, 16 * (chunk + 1))
                    for g in range(G):
                        dh, t = g // CT, g % CT
                        part = y[:, t, dh * BANK:(dh + 1) * BANK]
                        dve.wait_ge(y_done, it * G + g + 1)
                        dve.wait_ge(y_added, it * G + g - (G - 1) if not isinstance(it, int) else
                                    max(it * G + g - (G - 1), 0))
                        dve.tensor_tensor(part, banks[:, g % 8, :], part, ALU.add).then_inc(y_added, 1)

                blocks(dve, body)

            @block.tensor
            def _(pe):
                def body(b, it, chunk):
                    for j in range(FT):
                        pe.wait_ge(w1_lo_set, it * W1N + j + 1)
                        for n in range(NH):
                            e = j * NH + n
                            if chunk is not None and j == 0:
                                pe.wait_ge(u_loaded[n], 32 * (chunk + 1))
                            if not static(it, 0):
                                pe.wait_ge(y_added, it * G - 8 + e + 1)
                            for kt in range(KT):
                                for w, u in ((w1_hi, u_hi), (w1_hi, u_lo), (w1_lo, u_hi)):
                                    last = pe.matmul(banks[:, e, :], w[:, j % 2, kt, :],
                                                     u[:, n * TPB:(n + 1) * TPB, kt, :],
                                                     start=(kt == 0 and w is w1_hi and u is u_hi),
                                                     stop=(kt == KT - 1 and w is w1_lo))
                            last.then_inc(hid_done, 1)
                    for g in range(G):
                        dh, t = g // CT, g % CT
                        if t == 0:
                            pe.wait_ge(w2_lo_set, it * W2N + 2 * dh + 2)
                        if dh == 0 and t % TPB == 0:
                            pe.wait_ge(hid_lo_set, it * E + E - NH + t // TPB + 1)
                        if g < 8:
                            pe.wait_ge(sq_set, it * E + g + 1)
                        else:
                            pe.wait_ge(y_added, it * G + g - 8 + 1)
                        for j in range(FT):
                            for a, w in ((hid_hi, w2_hi), (hid_hi, w2_lo), (hid_lo, w2_hi)):
                                last = pe.matmul(banks[:, g % 8, :], a[:, j, t * P:(t + 1) * P], w[:, dh, j, :],
                                                 start=(j == 0 and a is hid_hi and w is w2_hi),
                                                 stop=(j == FT - 1 and a is hid_lo))
                        last.then_inc(y_done, 1)

                blocks(pe, body)


def build_program(nc, x, norm1_g, norm2_g, a_w_in, a_q_norm_g, a_k_norm_g, a_lambda_q1, a_lambda_k1,
                  a_lambda_q2, a_lambda_k2, a_subln_g, a_w_out, mlp_w1, mlp_w2, out):
    scratch = nc.dram_tensor("rows_scratch", [2, S, D], F32).ap()
    h_dram, o_dram = scratch[0], scratch[1]
    u2_dram = nc.dram_tensor("u2_scratch", [2, S, D], F32).ap()
    attention_steps(nc, x[0], norm1_g, a_w_in[0], a_q_norm_g, a_k_norm_g,
                    [a_lambda_q1, a_lambda_k1, a_lambda_q2, a_lambda_k2], o_dram)
    output_step(nc, x[0], o_dram, a_w_out[0], a_subln_g, norm2_g, h_dram, u2_dram)
    mlp_step(nc, h_dram, u2_dram, mlp_w1[0], mlp_w2[0], out[0])


_INS = ["x", "norm1_g", "norm2_g", "a_w_in", "a_q_norm_g", "a_k_norm_g", "a_lambda_q1", "a_lambda_k1",
        "a_lambda_q2", "a_lambda_k2", "a_subln_g", "a_w_out", "mlp_w1", "mlp_w2"]


def kernel(**inputs):
    import numpy as _np
    import concourse.bacc as _bacc
    from concourse.bass_utils import run_bass_kernel_spmd as _run

    nc = _bacc.Bacc("TRN2", target_bir_lowering=False, num_devices=1)
    arrays, args = {}, []
    for name in _INS:
        a = _np.ascontiguousarray(inputs[name])
        arrays[f"in_{name}"] = a
        args.append(nc.dram_tensor(f"in_{name}", a.shape, mybir.dt.from_np(a.dtype), kind="ExternalInput").ap())
    out = nc.dram_tensor("out", (1, S, D), F32, kind="ExternalOutput").ap()
    build_program(nc, *args, out)
    r = _run(nc, [arrays], core_ids=[0])
    return r.results[0]["out"]
```

```python
from contextlib import ExitStack

import concourse.bass as bass
from concourse import mybir

F32 = mybir.dt.float32
F32R = mybir.dt.float32r
BF16 = mybir.dt.bfloat16
ACT = mybir.ActivationFunctionType
ALU = mybir.AluOpType
AX = mybir.AxisListType

P = 128
S, D, DFF = 2048, 1024, 4096
H, DH = 8, 64
HD = 2 * DH
NT = S // P
KT = D // P
HALF = KT // 2
BANK = 512
TPB = BANK // P
EPS = 1e-6
SCALE = DH ** -0.5
LAMBDA_INIT = 0.2
MASKED = -1e30



def banks_of(j):
    return (NT - 1 - j) // TPB + 1


def groups_before(j):
    return sum(banks_of(i) for i in range(j))


def bank_order(j):
    return list(reversed(range(banks_of(j))))


def early_banks(j):
    return bank_order(j)[:max(banks_of(j - 2) - 2, 0)] if 2 <= j < NT else []


def late_banks(j):
    return bank_order(j)[len(early_banks(j)):]


def bank_width(j, bank):
    return min(BANK, (NT - j) * P - bank * BANK)


GROUPS = groups_before(NT)


def banks_of_tile(j):
    return banks_of(j % NT)


def group_index(j, n):
    return groups_before(j % NT) + n - (GROUPS if j < 0 else 0)


def pool_norms(j):
    return banks_of(j) > 2


SCORED = 2 * GROUPS


def score_index(j, m, n):
    return 2 * groups_before(j) + m * banks_of(j) + n


FIRST, MIDDLE, LAST, END = "first", "middle", "last", "end"


def turn_order(kind):
    order = []
    for j in range({END: 1}.get(kind, NT)):
        qk = [("qk", j - 1)] if kind in ((FIRST, MIDDLE) if j else (MIDDLE, LAST)) else []
        p = [("p", j - 1, n) for n in range(banks_of_tile(j - 1))] if kind != FIRST or j else []
        order += p[:1] + qk + p[1:] if j else qk + p
    return order


CT = 8
CHUNKS = NT // CT
FT = 4


def positive(value):
    return not (isinstance(value, int) and value <= 0)


def attention_steps(nc, x, norm1_g, w_in, q_g, k_g, lambdas, w_out, o_dram, u_t, w_out_raw, w_out_hi, w_out_lo):
    with ExitStack() as ctx:
        def sb(name, shape, dt=F32):
            return ctx.enter_context(nc.sbuf_tensor(name, shape, dt))

        def ps(name, shape):
            return ctx.enter_context(nc.psum_tensor(name, shape, F32))

        def sem(name):
            return ctx.enter_context(nc.semaphore(name))

        u_hi = sb("u_hi", [P, KT, P], F32R)
        u_lo = sb("u_lo", [P, KT, P], F32R)
        w_raw = sb("w_raw", [P, 2, 2, 3, HD])
        w_hi = sb("w_hi", [P, KT, 3 * HD], F32R)
        w_lo = sb("w_lo", [P, KT, 3 * HD], F32R)
        q_s = sb("q_s", [P, 2, S], F32R)
        k_hi = sb("k_hi", [P, 2, S], F32R)
        k_lo = sb("k_lo", [P, 2, S], F32R)
        v_s = sb("v_s", [P, NT, 2 * HD], F32R)
        p_all = sb("p_all", [P, 3, S])
        p1 = p_all[:, 2, :]
        pt_hi = sb("pt_hi", [P, 2, BANK], F32R)
        pt_lo = sb("pt_lo", [P, 2, BANK], F32R)
        qkv = sb("qkv", [P, 2, 3 * HD])
        qk_sq = sb("qk_sq", [P, 4 * DH])
        qk_ss = sb("qk_ss", [P, 4])
        qk_var = sb("qk_var", [P, 4])
        qk_rs = sb("qk_rs", [P, 4])
        qk_nat = sb("qk_nat", [P, 4, 2, DH])
        ident = sb("ident", [P, P])
        mask_l = sb("mask_l", [P, P], BF16)
        mask_r = sb("mask_r", [P, DH], BF16)
        g_q_raw = sb("g_q_raw", [P, 1])
        g_q = sb("g_q", [P, 1])
        g_k = sb("g_k", [P, 1])
        lam_v = qk_sq.rearrange("p (a d) -> p a d", a=4)
        lam_w = qkv[:, 0, 0:2 * DH].rearrange("p (a d) -> p a d", a=2)
        lam_s = sb("lam_s", [P, 2])
        lam_e = sb("lam_e", [P, 2])
        lam_d = sb("lam_d", [P, 1])
        neg_lam = sb("neg_lam", [P, 1])
        minus_half = sb("minus_half", [P, 4])
        eps = sb("eps", [P, 4])
        mx = sb("mx", [P, 2, 2, TPB])
        bias = sb("bias", [P, 2, 2])
        z_part = sb("z_part", [P, 2, 2, TPB])
        z = sb("z", [P, 2, 2])
        rz = sb("rz", [P, 2, 2])
        neg_c = sb("neg_c", [P, 2])
        o_tmp = sb("o_tmp", [P, 2, HD])
        o_sum = sb("o_sum", [P, 2, HD])
        o_ss = sb("o_ss", [P, 2])
        o_var = sb("o_var", [P, 2])
        o_rs = sb("o_rs", [P, 2])
        x_ss = sb("x_ss", [P, 2])
        x_var = sb("x_var", [P, 2])
        x_rs = sb("x_rs", [P, 2])
        x_in = p_all[:, 0, :].rearrange("p (a d) -> p a d", a=2)
        u_nat = p_all[:, 1, :].rearrange("p (a d) -> p a d", a=2)
        g1_row = p_all[:, 2, 0:D]
        x_junk = p_all[:, 2, D:2 * D]

        scores = ps("scores", [P, 4, BANK])
        turn = ps("turn", [P, 2, BANK])
        o_acc = ps("o_acc", [P, BANK])
        proj = ps("proj", [P, BANK])

        g1_loaded = sem("g1_loaded")
        consts_loaded, ident_set, consts_set = sem("consts_loaded"), sem("ident_set"), sem("consts_set")
        lam_step = sem("lam_step")
        x_loaded = [sem("x_loaded0"), sem("x_loaded1")]
        x_squared, x_var_set, x_rs_set = sem("x_squared"), sem("x_var_set"), sem("x_rs_set")
        u_normed, u_turned, u_kept = sem("u_normed"), sem("u_turned"), sem("u_kept")
        w_loaded = [sem("w_loaded0"), sem("w_loaded1")]
        w_hi_set, w_lo_set = sem("w_hi_set"), [sem("w_lo_set0"), sem("w_lo_set1")]
        u_hi_set, u_lo_set = sem("u_hi_set"), sem("u_lo_set")
        proj_half, qkv_kept = sem("proj_half"), sem("qkv_kept")
        qk_squared, qk_summed, qk_var_set, qk_rs_set = (
            sem("qk_squared"), sem("qk_summed"), sem("qk_var_set"), sem("qk_rs_set"))
        v_hi_set, v_lo_set, qk_normed, qk_turned = (
            sem("v_hi_set"), sem("v_lo_set"), sem("qk_normed"), sem("qk_turned"))
        q_hi_set, k_hi_set, q_lo_set, k_lo_set = (
            sem("q_hi_set"), sem("k_hi_set"), sem("q_lo_set"), sem("k_lo_set"))
        scored, bank_max, bias_set, exp_done = (
            sem("scored"), sem("bank_max"), sem("bias_set"), sem("exp_done"))
        z_summed, z_inverted, c_set = sem("z_summed"), sem("z_inverted"), sem("c_set")
        combined = sem("combined")
        p_turned, pt_hi_set, pt_lo_set, pv_done = (
            sem("p_turned"), sem("pt_hi_set"), sem("pt_lo_set"), sem("pv_done"))
        o_low_set, o_summed, o_squared, o_var_set, o_rs_set, o_normed = (
            sem("o_low_set"), sem("o_summed"), sem("o_squared"), sem("o_var_set"),
            sem("o_rs_set"), sem("o_normed"))
        o_stored = [sem("o_stored0"), sem("o_stored1")]
        w_out_loaded, w_out_hi_set, w_out_lo_set = sem("w_out_loaded"), sem("w_out_hi_set"), sem("w_out_lo_set")

        w_view = w_in.rearrange("(kt p) (s c) -> p kt s c", p=P, s=3)

        def load_weights(sp, hp, pieces=range(4)):
            cols = bass.ds(hp * HD if isinstance(hp, int) else sp.snap(hp * HD), HD)
            for n in pieces:
                if positive(hp * 2 + n // 2):
                    sp.wait_ge(w_lo_set[n % 2], hp * 2 + n // 2)
                for s in range(3):
                    sp.dma_start(w_raw[:, n % 2, :, s, :],
                                 w_view[:, 2 * n:2 * n + 2, s, cols])\
                      .then_inc(w_loaded[n % 2], 16)

        def raw_piece(n):
            return w_raw[:, n % 2].rearrange("p a s c -> p (a s c)")

        def w_piece(w, n):
            return w[:, 2 * n:2 * n + 2, :].rearrange("p a c -> p (a c)")

        def act_split_weights(act, hp, pieces=range(4)):
            if positive(hp):
                act.wait_ge(proj_half, hp * 2 * NT)
            for n in pieces:
                act.wait_ge(w_loaded[n % 2], (hp * 2 + n // 2 + 1) * 48)
                act.activation(w_piece(w_hi, n), raw_piece(n), ACT.Copy).then_inc(w_hi_set, 1)

        def low_weights(engine, hp, n):
            engine.wait_ge(w_hi_set, hp * 4 + n + 1)
            engine.tensor_tensor(w_piece(w_lo, n), raw_piece(n), w_piece(w_hi, n).bitcast(F32), ALU.subtract)\
                .then_inc(w_lo_set[n % 2], 1)

        def act_split_u(act, hp, j, half):
            t, n = NT - 1 - j, hp * NT + j
            kts = slice(half * HALF, (half + 1) * HALF)
            if positive(2 * n + half - 1):
                act.wait_ge(proj_half, 2 * n + half - 1)
            act.activation(u_hi[:, kts, :], u_t[:, t, kts, :], ACT.Copy).then_inc(u_hi_set, 1)

        def pool_split_u(pool, hp, j, half):
            t, n = NT - 1 - j, hp * NT + j
            kts = slice(half * HALF, (half + 1) * HALF)
            pool.wait_ge(u_hi_set, 2 * n + half + 1)
            pool.tensor_tensor(u_lo[:, kts, :], u_t[:, t, kts, :], u_hi[:, kts, :].bitcast(F32), ALU.subtract)\
                .then_inc(u_lo_set, 1)

        def pe_project(pe, hp, j, half):
            n = hp * NT + j
            if half == 0 and positive(n):
                pe.wait_ge(qkv_kept, n)
            if j == 0:
                for slot in range(2):
                    pe.wait_ge(w_lo_set[slot], hp * 2 + 1 + half)
            pe.wait_ge(u_lo_set, 2 * n + half + 1)
            for kt in range(half * HALF, (half + 1) * HALF):
                for a, w in ((u_hi, w_hi), (u_hi, w_lo), (u_lo, w_hi)):
                    last = pe.matmul(proj[:, 0:3 * HD], a[:, kt, :], w[:, kt, :],
                                     start=(kt == 0 and a is u_hi and w is w_hi),
                                     stop=(kt == KT - 1 and a is u_lo))
            last.then_inc(proj_half, 1)

        def act_keep_qkv(act, hp, j):
            n = hp * NT + j
            act.wait_ge(proj_half, 2 * n + 2)
            if positive(n - 1):
                act.wait_ge(qk_normed, n - 1)
                act.wait_ge(v_lo_set, n - 1)
            act.activation(qkv[:, j % 2, :], proj[:, 0:3 * HD], ACT.Copy).then_inc(qkv_kept, 1)

        def act_square_qk(act, hp, j):
            n = hp * NT + j
            act.wait_ge(qkv_kept, n + 1)
            if positive(n):
                act.wait_ge(qk_summed, n)
            act.activation(qk_sq[:, :], qkv[:, j % 2, 0:2 * HD], ACT.Square, scale=DH ** -0.5)\
               .then_inc(qk_squared, 1)

        def act_v(act, hp, j):
            t = NT - 1 - j % NT
            if not (isinstance(hp, int) and hp == 0):
                act.wait_ge(pv_done, (hp - 1) * GROUPS + group_index(j, banks_of_tile(j)))
            act.activation(v_s[:, t, 0:HD], qkv[:, j % 2, 2 * HD:3 * HD], ACT.Copy).then_inc(v_hi_set, 1)

        def low_v(engine, hp, j):
            t, n = NT - 1 - j % NT, hp * NT + j
            engine.wait_ge(v_hi_set, n + 1)
            engine.tensor_tensor(v_s[:, t, HD:2 * HD], qkv[:, j % 2, 2 * HD:3 * HD],
                                 v_s[:, t, 0:HD].bitcast(F32), ALU.subtract).then_inc(v_lo_set, 1)

        def dve_sum_qk(dve, hp, j):
            n = hp * NT + j
            dve.wait_ge(qk_squared, n + 1)
            if positive(n):
                dve.wait_ge(qk_var_set, n)
            dve.tensor_reduce(qk_ss[:, :], qk_sq[:, :].rearrange("p (g d) -> p g d", g=4), AX.X, ALU.add)\
               .then_inc(qk_summed, 1)

        def pool_project(pool, hp, j):
            n = hp * NT + j
            pool.wait_ge(qk_summed, n + 1)
            if positive(n):
                pool.wait_ge(qk_rs_set, n)
            pool.tensor_tensor(qk_var[:, :], qk_ss[:, :], eps[:, :], ALU.add).then_inc(qk_var_set, 1)
            pool.wait_ge(qk_var_set, n + 1)
            if positive(n):
                pool.wait_ge(qk_normed, n)
            pool.tensor_tensor(qk_rs[:, :], qk_var[:, :], minus_half[:, :], ALU.pow).then_inc(qk_rs_set, 1)

        def norm_qk(engine, hp, j):
            n = hp * NT + j
            engine.wait_ge(qk_rs_set, n + 1)
            if positive(n):
                engine.wait_ge(qk_turned, n)
            engine.tensor_tensor(
                qk_nat[:, :, :, :],
                qkv[:, j % 2, 0:2 * HD].rearrange("p (g d) -> p g d", g=4).unsqueeze(2)
                .to_broadcast([P, 4, 2, DH]),
                qk_rs[:, :].unsqueeze(2).unsqueeze(3).to_broadcast([P, 4, 2, DH]),
                ALU.mult).then_inc(qk_normed, 1)

        def pe_turn_qk(pe, hp, j, slot):
            n = hp * NT + j
            pe.wait_ge(qk_normed, n + 1)
            for g in range(4):
                last = pe.transpose(turn[:, slot, g * P:(g + 1) * P],
                                    qk_nat[:, g, :, :].rearrange("p a d -> p (a d)"), ident[:, :])
            last.then_inc(qk_turned, 1)

        def turned(slot, g, rows=slice(0, P)):
            return turn[rows, slot, g * 2 * P:(g + 1) * 2 * P].rearrange("p (m r) -> p m r", m=2)

        def act_turned_qk(act, hp, j, slot):
            t, n = NT - 1 - j % NT, hp * NT + j
            rows = slice(t * P, (t + 1) * P)
            act.wait_ge(qk_turned, n + 1)
            if not (isinstance(hp, int) and hp == 0):
                act.wait_ge(scored, (hp - 1) * SCORED + 2 * group_index(j, banks_of_tile(j)))
            act.activation(k_hi[:, :, rows], turned(slot, 1), ACT.Copy, scale=g_k[:, :]).then_inc(k_hi_set, 1)
            act.activation(q_s[:, :, rows], turned(slot, 0), ACT.Copy, scale=g_q[:, :]).then_inc(q_hi_set, 1)

        def dve_turned_qk(dve, hp, j, slot):
            t, n = NT - 1 - j % NT, hp * NT + j
            rows, low = slice(t * P, (t + 1) * P), slice(DH, P)
            dve.wait_ge(q_hi_set, n + 1)
            dve.scalar_tensor_tensor(k_lo[:, :, rows], turned(slot, 1), g_k[:, :],
                                     k_hi[:, :, rows].bitcast(F32), ALU.mult, ALU.subtract)\
               .then_inc(k_lo_set, 1)
            dve.scalar_tensor_tensor(q_s[low, :, rows], turned(slot, 0, low), g_q[low, :],
                                     q_s[low, :, rows].bitcast(F32), ALU.mult, ALU.subtract)\
               .then_inc(q_lo_set, 1)

        with nc.Block() as block:
            @block.sync
            def _(sp):
                for j in range(2):
                    sp.dma_start(x_in[:, j, :], x[(NT - 1 - j) * P:(NT - j) * P, :]).then_inc(x_loaded[j], 16)
                sp.dma_start(g1_row, norm1_g.to_broadcast([P, D])).then_inc(g1_loaded, 16)
                load_weights(sp, 0, (0, 1))
                with nc.allow_non_contiguous_dma("gains and lambdas, once"):
                    for half in range(2):
                        sp.dma_start(g_q_raw[half * DH:(half + 1) * DH, :], q_g.rearrange("a d -> d a"))\
                          .then_inc(consts_loaded, 16)
                        sp.dma_start(g_k[half * DH:(half + 1) * DH, :], k_g.rearrange("a d -> d a"))\
                          .then_inc(consts_loaded, 16)
                    for n, v in enumerate(lambdas):
                        sp.dma_start(lam_v[:, n, :], v.to_broadcast([P, DH])).then_inc(consts_loaded, 16)
                load_weights(sp, 0, (2, 3))
                for j in range(2, NT):
                    sp.wait_ge(u_normed, j - 1)
                    sp.dma_start(x_in[:, j % 2, :], x[(NT - 1 - j) * P:(NT - j) * P, :])\
                      .then_inc(x_loaded[j % 2], 16)

            @block.gpsimd
            def _(pool):
                pool.memset(ident[:, :], 0.0).then_inc(ident_set, 1)
                pool.wait_ge(ident_set, 1)
                pool.affine_select(out=ident[:, :], in_=ident[:, :], compare_op=ALU.not_equal, fill=1.0,
                                   base=0, pattern=[[-1, P]], channel_multiplier=1).then_inc(ident_set, 1)
                pool.memset(minus_half[:, :], -0.5).then_inc(ident_set, 1)
                pool.memset(eps[:, :], EPS).then_inc(ident_set, 1)

                def x_factor(j):
                    pool.wait_ge(x_squared, j + 1)
                    pool.tensor_tensor(x_var[:, j % 2:j % 2 + 1], x_ss[:, j % 2:j % 2 + 1], eps[:, 0:1], ALU.add)\
                        .then_inc(x_var_set, 1)
                    pool.wait_ge(x_var_set, j + 1)
                    if j >= 2:
                        pool.wait_ge(u_normed, j - 1)
                    pool.tensor_tensor(x_rs[:, j % 2:j % 2 + 1], x_var[:, j % 2:j % 2 + 1],
                                       minus_half[:, 0:1], ALU.pow).then_inc(x_rs_set, 1)

                pool.wait_ge(ident_set, 4)
                x_factor(0)
                x_factor(1)
                low_weights(pool, 0, 0)
                for half in range(2):
                    pool_split_u(pool, 0, 0, half)
                low_weights(pool, 0, 2)
                for j in range(NT):
                    if j + 2 < NT:
                        x_factor(j + 2)
                    if j + 1 < NT:
                        for half in range(2):
                            pool_split_u(pool, 0, j + 1, half)
                    pool_project(pool, 0, j)

            @block.scalar
            def _(act):
                def x_square(j):
                    act.wait_ge(x_loaded[j % 2], 16 * (j // 2 + 1))
                    if j >= 1:
                        act.wait_ge(x_squared, j)
                    if j >= 2:
                        act.wait_ge(x_var_set, j - 1)
                    act.activation(x_junk, x_in[:, j % 2, :], ACT.Square, scale=D ** -0.5,
                                   accum_out=x_ss[:, j % 2:j % 2 + 1]).then_inc(x_squared, 1)

                x_square(0)
                x_square(1)
                act_split_weights(act, 0, (0, 1))
                act.wait_ge(u_kept, 1)
                for half in range(2):
                    act_split_u(act, 0, 0, half)
                act.wait_ge(lam_step, 1)
                act.activation(lam_e[:, :], lam_s[:, :], ACT.Exp).then_inc(lam_step, 1)
                act_split_weights(act, 0, (2, 3))
                for j in range(NT):
                    if j + 2 < NT:
                        x_square(j + 2)
                    if j + 1 < NT:
                        act.wait_ge(u_kept, j + 2)
                        act_split_u(act, 0, j + 1, 0)
                    if j:
                        act_turned_qk(act, 0, j - 1, (j - 1) % 2)
                    act_keep_qkv(act, 0, j)
                    if j + 1 < NT:
                        act_split_u(act, 0, j + 1, 1)
                    act_square_qk(act, 0, j)
                    act_v(act, 0, j)
                act_turned_qk(act, 0, NT - 1, (NT - 1) % 2)

            @block.vector
            def _(dve):
                def u_norm(j):
                    dve.wait_ge(x_rs_set, j + 1)
                    if j >= 2:
                        dve.wait_ge(u_turned, j - 1)
                    dve.scalar_tensor_tensor(u_nat[:, j % 2, :], x_in[:, j % 2, :], x_rs[:, j % 2:j % 2 + 1],
                                             g1_row, ALU.mult, ALU.mult).then_inc(u_normed, 1)

                def u_keep(j):
                    dve.wait_ge(u_turned, j + 1)
                    dve.tensor_copy(u_t[:, NT - 1 - j, :, :].rearrange("p a b -> p (a b)"),
                                    scores[:, 2 * (j % 2):2 * (j % 2) + 2, :].rearrange("p a b -> p (a b)"))\
                       .then_inc(u_kept, 1)

                for par in range(2):
                    dve.memset(o_sum[:, par, :], 0.0).then_inc(o_stored[par], 16)
                dve.wait_ge(g1_loaded, 16)
                u_norm(0)
                u_norm(1)
                u_keep(0)
                low_weights(dve, 0, 1)
                dve.memset(mask_l[:, :], 0.0).then_inc(consts_set, 1)
                dve.memset(mask_r[:, :], 0.0).then_inc(consts_set, 1)
                dve.wait_ge(consts_set, 2)
                dve.memset(mask_l[0:1, 0:DH], 1.0).then_inc(consts_set, 1)
                dve.memset(mask_r[0:1, :], MASKED).then_inc(consts_set, 1)
                dve.wait_ge(consts_loaded, 16 * 8)
                dve.tensor_tensor(lam_w[:, :, :], lam_v[:, 0::2, :], lam_v[:, 1::2, :], ALU.mult)\
                   .then_inc(consts_set, 1)
                dve.tensor_scalar(g_q[:, :], g_q_raw[:, :], SCALE, None, ALU.mult).then_inc(consts_set, 1)
                dve.wait_ge(consts_set, 6)
                dve.tensor_reduce(lam_s[:, :], lam_w[:, :, :], AX.X, ALU.add).then_inc(lam_step, 1)
                dve.wait_ge(lam_step, 2)
                dve.tensor_tensor(lam_d[:, :], lam_e[:, 1:2], lam_e[:, 0:1], ALU.subtract).then_inc(lam_step, 1)
                dve.wait_ge(lam_step, 3)
                dve.tensor_scalar(neg_lam[:, :], lam_d[:, :], LAMBDA_INIT, None, ALU.subtract)\
                   .then_inc(lam_step, 1)
                low_weights(dve, 0, 3)
                for j in range(NT):
                    if j + 1 < NT:
                        u_keep(j + 1)
                    if j:
                        norm_qk(dve, 0, j - 1)
                    if j + 2 < NT:
                        u_norm(j + 2)
                    if j:
                        dve_turned_qk(dve, 0, j - 1, (j - 1) % 2)
                    dve_sum_qk(dve, 0, j)
                    low_v(dve, 0, j)
                norm_qk(dve, 0, NT - 1)
                dve_turned_qk(dve, 0, NT - 1, (NT - 1) % 2)

            @block.tensor
            def _(pe):
                def turn_u(j):
                    pe.wait_ge(u_normed, j + 1)
                    if j >= 2:
                        pe.wait_ge(u_kept, j - 1)
                    for kt in range(KT):
                        last = pe.transpose(scores[:, 2 * (j % 2) + kt // TPB, (kt % TPB) * P:(kt % TPB + 1) * P],
                                            u_nat[:, j % 2, kt * P:(kt + 1) * P], ident[:, :])
                    last.then_inc(u_turned, 1)

                def turn_qk(j):
                    if j >= 2:
                        pe.wait_ge(q_lo_set, j - 1)
                    pe_turn_qk(pe, 0, j, j % 2)

                pe.wait_ge(ident_set, 4)
                turn_u(0)
                for j in range(NT):
                    if j + 1 < NT:
                        turn_u(j + 1)
                    for half in range(2):
                        pe_project(pe, 0, j, half)
                    if j:
                        turn_qk(j - 1)
                turn_qk(NT - 1)

        fills = {kind: turn_order(kind) for kind in (FIRST, MIDDLE, LAST, END)}
        assert all(len(fills[kind]) % 2 == 0 for kind in (FIRST, MIDDLE)) and NT % 2 == 0
        fills[END] = ([None] if len(fills[LAST]) % 2 else []) + fills[END]

        def slot_of(kind, what):
            return fills[kind].index(what) % 2

        def wait_slot(pe, h, kind, what):
            at, order = fills[kind].index(what), fills[kind]
            if at < 2 and kind == FIRST:
                return
            if at < 2:
                order = [(w[0], w[1] - NT) + w[2:] for w in fills[LAST if kind == END else MIDDLE][-2:]]
                if kind == END and None in fills[END]:
                    at -= 1
                last = order[at]
            else:
                last = order[at - 2]
            if last[0] == "p":
                pe.wait_ge(pt_lo_set, h * GROUPS + group_index(last[1], last[2]) + 1)
            else:
                pe.wait_ge(q_lo_set, (h + 1) * NT + last[1] + 1)

        def pe_scores(pe, h, j, m, banks):
            t = NT - 1 - j
            for bank in banks:
                n = bank_order(j).index(bank)
                if m == 1:
                    pe.wait_ge(exp_done, h * SCORED + score_index(j, 0, n) + 1)
                elif j:
                    before = bank_order(j - 1).index(bank)
                    pe.wait_ge(exp_done, h * SCORED + score_index(j - 1, 1, before) + 1)
                else:
                    pe.wait_ge(k_lo_set, h * NT + NT - TPB * bank)
                    if n == 0:
                        pe.wait_ge(q_lo_set, h * NT + 1)
                width = bank_width(j, bank)
                q = q_s[:, m, t * P:(t + 1) * P]
                keys = slice(bank * BANK, bank * BANK + width)
                masked = bank == banks_of(j) - 1
                if masked:
                    pe.matmul(scores[:, bank, width - DH:width], mask_l[:, :], mask_r[:, :],
                              start=True, stop=False, skip_group_check=True)
                pe.matmul(scores[:, bank, 0:width], q, k_hi[:, m, keys], start=not masked, stop=False,
                          skip_group_check=True)
                last = pe.matmul(scores[:, bank, 0:width], q, k_lo[:, m, keys], start=False, stop=True,
                                 skip_group_check=True)
                last.then_inc(scored, 1)

        def dve_max(dve, h, j, m, banks):
            par = j % 2
            for bank in banks:
                n = bank_order(j).index(bank)
                dve.wait_ge(scored, h * SCORED + score_index(j, m, n) + 1)
                dve.tensor_reduce(mx[:, par, m, n:n + 1], scores[:, bank, 0:bank_width(j, bank)], AX.X, ALU.max)\
                   .then_inc(bank_max, 1)

        def dve_bias(dve, h, j, m):
            par, nb = j % 2, banks_of(j)
            dve.wait_ge(bank_max, h * SCORED + score_index(j, m, nb))
            dve.tensor_reduce(bias[:, par, m:m + 1], mx[:, par, m, 0:nb], AX.X, ALU.max, negate=True)\
               .then_inc(bias_set, 1)

        def act_exps(act, h, j, m, banks):
            par = j % 2
            if banks[0] == banks_of(j) - 1:
                act.wait_ge(bias_set, h * 2 * NT + 2 * j + m + 1)
                if m == 0 and positive(h * GROUPS + group_index(j - 1, 0)):
                    act.wait_ge(p_turned, h * GROUPS + group_index(j - 1, 0))
                if m == 1 and positive(h * GROUPS + groups_before(j)):
                    act.wait_ge(combined, h * GROUPS + groups_before(j))
            for bank in banks:
                n, width = bank_order(j).index(bank), bank_width(j, bank)
                dst = (p_all[:, par, :] if m == 0 else p1)[:, bank * BANK:bank * BANK + width]
                act.activation(dst, scores[:, bank, 0:width], ACT.Exp, bias=bias[:, par, m:m + 1],
                               accum_out=z_part[:, par, m, n:n + 1]).then_inc(exp_done, 1)

        def group_columns(j, n):
            bank = bank_order(j % NT)[n]
            return slice(bank * BANK, bank * BANK + bank_width(j % NT, bank))

        def dve_coefficient(dve, h, j):
            par, nb = j % 2, banks_of_tile(j)
            dve.wait_ge(exp_done, h * SCORED + 2 * group_index(j, nb))
            dve.tensor_reduce(z[:, par, :], z_part[:, par, :, 0:nb], AX.X, ALU.add).then_inc(z_summed, 1)
            dve.wait_ge(z_summed, h * NT + j + 1)
            dve.reciprocal(rz[:, par, :], z[:, par, :]).then_inc(z_inverted, 1)
            dve.wait_ge(z_inverted, h * NT + j + 1)
            dve.tensor_scalar(neg_c[:, par:par + 1], z[:, par, 0:1], rz[:, par, 1:2], neg_lam[:, :],
                              ALU.mult, ALU.mult).then_inc(c_set, 1)

        def dve_combine(dve, h, j):
            par = j % 2
            dve.wait_ge(c_set, h * NT + j + 1)
            for bank in bank_order(j % NT):
                cols = slice(bank * BANK, bank * BANK + bank_width(j % NT, bank))
                dve.scalar_tensor_tensor(p_all[:, par, cols], p1[:, cols], neg_c[:, par:par + 1],
                                         p_all[:, par, cols], ALU.mult, ALU.add).then_inc(combined, 1)

        def pe_turn_p(pe, h, kind, j, n):
            bank = bank_order(j % NT)[n]
            pe.wait_ge(combined, h * GROUPS + group_index(j, n) + 1)
            wait_slot(pe, h, kind, ("p", j, n))
            slot = slot_of(kind, ("p", j, n))
            for c in range(bank_width(j % NT, bank) // P):
                at = bank * BANK + c * P
                last = pe.transpose(turn[:, slot, c * P:(c + 1) * P], p_all[:, j % 2, at:at + P], ident[:, :])
            last.then_inc(p_turned, 1)

        def act_turned_p(act, h, kind, j, n):
            g = group_index(j, n)
            width = bank_width(j % NT, bank_order(j % NT)[n])
            act.wait_ge(p_turned, h * GROUPS + g + 1)
            if positive(h * GROUPS + g - 1):
                act.wait_ge(pv_done, h * GROUPS + g - 1)
            act.activation(pt_hi[:, g % 2, 0:width], turn[:, slot_of(kind, ("p", j, n)), 0:width], ACT.Copy)\
               .then_inc(pt_hi_set, 1)

        def dve_turned_p(dve, h, kind, j, n):
            g = group_index(j, n)
            width = bank_width(j % NT, bank_order(j % NT)[n])
            dve.wait_ge(pt_hi_set, h * GROUPS + g + 1)
            dve.tensor_tensor(pt_lo[:, g % 2, 0:width], turn[:, slot_of(kind, ("p", j, n)), 0:width],
                              pt_hi[:, g % 2, 0:width].bitcast(F32), ALU.subtract).then_inc(pt_lo_set, 1)

        def pe_values(pe, h, j, n):
            g, bank, nb = group_index(j, n), bank_order(j % NT)[n], banks_of_tile(j)
            tiles = bank_width(j % NT, bank) // P
            if n == 0 and positive(h * NT + j):
                pe.wait_ge(o_summed, h * NT + j)
            if j == 0:
                pe.wait_ge(v_lo_set, h * NT + NT - TPB * bank)
            pe.wait_ge(pt_lo_set, h * GROUPS + g + 1)
            for c in range(tiles):
                v = v_s[:, bank * TPB + c, :]
                pe.matmul(o_acc[:, 0:2 * HD], pt_hi[:, g % 2, c * P:(c + 1) * P], v, start=(n == 0 and c == 0),
                          stop=False, skip_group_check=True)
                last = pe.matmul(o_acc[:, 0:HD], pt_lo[:, g % 2, c * P:(c + 1) * P], v[:, 0:HD], start=False,
                                 stop=(n == nb - 1 and c == tiles - 1), skip_group_check=True)
            last.then_inc(pv_done, 1)

        def act_output_low(act, h, j):
            par, a = j % 2, h * NT + j
            act.wait_ge(pv_done, h * GROUPS + group_index(j, banks_of_tile(j)))
            act.wait_ge(z_inverted, a + 1)
            act.activation(o_tmp[:, par, :], o_acc[:, HD:2 * HD], ACT.Copy, scale=rz[:, par, 0:1])\
               .then_inc(o_low_set, 1)

        def dve_output(dve, h, j):
            par, a = j % 2, h * NT + j
            dve.wait_ge(o_low_set, a + 1)
            dve.wait_ge(o_stored[par], 16 * (h * (NT // 2) + j // 2 + 1))
            dve.scalar_tensor_tensor(o_sum[:, par, :], o_acc[:, 0:HD], rz[:, par, 0:1], o_tmp[:, par, :],
                                     ALU.mult, ALU.add).then_inc(o_summed, 1)

        def act_square_output(act, h, j):
            par, a = j % 2, h * NT + j
            act.wait_ge(o_summed, a + 1)
            act.activation(o_tmp[:, par, :], o_sum[:, par, :], ACT.Square, scale=HD ** -0.5,
                           accum_out=o_ss[:, par:par + 1])\
               .then_inc(o_squared, 1)

        def pool_output(pool, h, j):
            par, a = j % 2, h * NT + j
            pool.wait_ge(o_squared, a + 1)
            pool.tensor_tensor(o_var[:, par:par + 1], o_ss[:, par:par + 1], eps[:, 0:1], ALU.add)\
                .then_inc(o_var_set, 1)
            pool.wait_ge(o_var_set, a + 1)
            pool.tensor_tensor(o_rs[:, par:par + 1], o_var[:, par:par + 1], minus_half[:, 0:1], ALU.pow)\
                .then_inc(o_rs_set, 1)

        def act_norm_output(act, h, j):
            par, a = j % 2, h * NT + j
            act.wait_ge(o_rs_set, a + 1)
            act.activation(o_sum[:, par, :], o_sum[:, par, :], ACT.Copy, scale=o_rs[:, par:par + 1])\
               .then_inc(o_normed, 1)

        def store_outputs(sp, h, tiles):
            cols = bass.ds(h * HD if isinstance(h, int) else sp.snap(h * HD), HD)
            for j in tiles:
                t = NT - 1 - j
                sp.wait_ge(o_normed, h * NT + j + 1)
                sp.dma_start(o_dram[t * P:(t + 1) * P, cols], o_sum[:, j % 2, :])\
                  .then_inc(o_stored[j % 2], 16)

        def run_heads(engine, head):
            head(0, FIRST)
            with engine.Fori(1, H - 1) as h:
                head(h, MIDDLE)
            head(H - 1, LAST)
            head(H, END)

        def steps(kind):
            for j in range(2 if kind == END else NT):
                scoring, projecting = kind != END, kind in (FIRST, MIDDLE)
                yield (j, scoring, projecting,
                       projecting if j else kind in (MIDDLE, LAST),
                       kind != FIRST if j == 0 else kind != END,
                       kind != FIRST or j >= 2)

        def pe_head(pe, h, kind):
            for j, scoring, projecting, projected, one_back, two_back in steps(kind):
                order = bank_order(j)

                def turn_qk():
                    wait_slot(pe, h, kind, ("qk", j - 1))
                    pe_turn_qk(pe, h + 1, j - 1, slot_of(kind, ("qk", j - 1)))

                if scoring:
                    pe_scores(pe, h, j, 0, late_banks(j) if j else order[:-1])
                if two_back:
                    pe_values(pe, h, j - 2, banks_of_tile(j - 2) - 1)
                if projected and j == 0:
                    turn_qk()
                if scoring and j == 0:
                    pe_scores(pe, h, j, 0, order[-1:])
                if projecting:
                    pe_project(pe, h + 1, j, 0)
                if one_back:
                    pe_turn_p(pe, h, kind, j - 1, 0)
                if scoring:
                    pe_scores(pe, h, j, 1, order)
                if projected and j:
                    turn_qk()
                if projecting:
                    pe_project(pe, h + 1, j, 1)
                if one_back:
                    for n in range(1, banks_of_tile(j - 1)):
                        pe_turn_p(pe, h, kind, j - 1, n)
                        if scoring and n >= 2:
                            pe_scores(pe, h, j + 1, 0, early_banks(j + 1)[n - 2:n - 1])
                        pe_values(pe, h, j - 1, n - 1)

        def act_head(act, h, kind):
            for j, scoring, projecting, projected, one_back, two_back in steps(kind):
                nb = banks_of_tile(j - 1)
                order = bank_order(j)
                if projecting and j == 0:
                    act_split_weights(act, h + 1, (0, 1))
                if two_back:
                    act_output_low(act, h, j - 2)
                if projecting and j == 0:
                    for half in range(2):
                        act_split_u(act, h + 1, 0, half)
                if projected and j == 0:
                    act_turned_qk(act, h + 1, j - 1, slot_of(kind, ("qk", j - 1)))
                if projecting and j == 0:
                    act_split_weights(act, h + 1, (2,))
                if scoring:
                    act_exps(act, h, j, 0, order)
                if projecting and j == 0:
                    act_split_weights(act, h + 1, (3,))
                if one_back:
                    act_turned_p(act, h, kind, j - 1, 0)
                if two_back:
                    act_square_output(act, h, j - 2)
                if two_back and (kind in (FIRST, MIDDLE) or (kind == LAST and j < 2)):
                    act_v(act, h + 1, j - 2)
                if projecting and j < NT - 1:
                    act_split_u(act, h + 1, j + 1, 0)
                if projected and j:
                    act_turned_qk(act, h + 1, j - 1, slot_of(kind, ("qk", j - 1)))
                if two_back:
                    act_norm_output(act, h, j - 2)
                if scoring:
                    act_exps(act, h, j, 1, order[:2])
                if projecting and j and nb <= 2:
                    act_keep_qkv(act, h + 1, j)
                    act_square_qk(act, h + 1, j)
                if one_back and nb > 1:
                    act_turned_p(act, h, kind, j - 1, 1)
                if scoring and order[2:]:
                    act_exps(act, h, j, 1, order[2:])
                if one_back and nb > 2:
                    act_turned_p(act, h, kind, j - 1, 2)
                if projecting and (j == 0 or nb > 2):
                    act_keep_qkv(act, h + 1, j)
                    act_square_qk(act, h + 1, j)
                if projecting and j < NT - 1:
                    act_split_u(act, h + 1, j + 1, 1)
                if one_back and nb > 3:
                    act_turned_p(act, h, kind, j - 1, 3)
                if kind == LAST and j >= NT - KT:
                    act.wait_ge(w_out_loaded, 16 * KT)
                    act.activation(w_out_hi[:, j - (NT - KT), :], w_out_raw[:, j - (NT - KT), :],
                                   ACT.Copy).then_inc(w_out_hi_set, 1)

        def dve_head(dve, h, kind):
            for j, scoring, projecting, projected, one_back, two_back in steps(kind):
                nb = banks_of_tile(j - 1)
                order = bank_order(j)
                if one_back and nb <= 3:
                    dve_coefficient(dve, h, j - 1)
                if scoring and j:
                    dve_max(dve, h, j, 0, late_banks(j))
                    dve_bias(dve, h, j, 0)
                if scoring and j == 0:
                    dve_max(dve, h, j, 0, order[:2])
                if j == 1 and projecting:
                    dve_sum_qk(dve, h + 1, 0)
                if projected and j == 0:
                    norm_qk(dve, h + 1, j - 1)
                if scoring and j == 0:
                    dve_max(dve, h, j, 0, order[2:-1])
                if projecting and j == 0:
                    low_weights(dve, h + 1, 1)
                if one_back and j:
                    if nb > 3:
                        dve_coefficient(dve, h, j - 1)
                    dve_combine(dve, h, j - 1)
                if two_back:
                    dve_output(dve, h, j - 2)
                if projected and j == 0:
                    dve_turned_qk(dve, h + 1, j - 1, slot_of(kind, ("qk", j - 1)))
                if scoring and j == 0:
                    dve_max(dve, h, j, 0, order[-1:])
                    dve_bias(dve, h, j, 0)
                if one_back and j == 0:
                    dve_combine(dve, h, j - 1)
                if projecting and j == 0:
                    low_weights(dve, h + 1, 3)
                if projected and j and not pool_norms(j - 1):
                    norm_qk(dve, h + 1, j - 1)
                if one_back and nb <= 2:
                    dve_turned_p(dve, h, kind, j - 1, 0)
                if scoring:
                    dve_max(dve, h, j, 1, order)
                    dve_bias(dve, h, j, 1)
                if one_back and nb > 2:
                    dve_turned_p(dve, h, kind, j - 1, 0)
                if projected and j:
                    dve_turned_qk(dve, h + 1, j - 1, slot_of(kind, ("qk", j - 1)))
                if projecting and j and nb <= 2:
                    dve_sum_qk(dve, h + 1, j)
                for n in range(1, min(nb, 3)):
                    if one_back:
                        dve_turned_p(dve, h, kind, j - 1, n)
                    if scoring:
                        dve_max(dve, h, j + 1, 0, early_banks(j + 1)[n - 1:n])
                if projecting and nb > 2:
                    dve_sum_qk(dve, h + 1, j)
                if one_back and nb > 3:
                    dve_turned_p(dve, h, kind, j - 1, 3)

        def pool_head(pool, h, kind):
            for j, scoring, projecting, projected, one_back, two_back in steps(kind):
                if projecting and j == 0:
                    low_weights(pool, h + 1, 0)
                    for half in range(2):
                        pool_split_u(pool, h + 1, 0, half)
                    low_weights(pool, h + 1, 2)
                if two_back:
                    pool_output(pool, h, j - 2)
                if two_back and (kind in (FIRST, MIDDLE) or (kind == LAST and j < 2)):
                    low_v(pool, h + 1, j - 2)
                if projecting and j < NT - 1:
                    pool_split_u(pool, h + 1, j + 1, 0)
                if projecting and j == 0:
                    pool_split_u(pool, h + 1, 1, 1)
                if projecting:
                    pool_project(pool, h + 1, j)
                    if pool_norms(j):
                        norm_qk(pool, h + 1, j)
                    if 0 < j < NT - 1:
                        pool_split_u(pool, h + 1, j + 1, 1)
                if kind == LAST and j >= NT - KT:
                    kt = j - (NT - KT)
                    pool.wait_ge(w_out_hi_set, kt + 1)
                    pool.tensor_tensor(w_out_lo[:, kt, :], w_out_raw[:, kt, :],
                                       w_out_hi[:, kt, :].bitcast(F32), ALU.subtract).then_inc(w_out_lo_set, 1)

        with nc.Block() as block:
            @block.sync
            def _(sp):
                half = NT // 2
                load_weights(sp, 1)
                store_outputs(sp, 0, range(half))
                with sp.Fori(1, H - 1) as h:
                    load_weights(sp, h + 1, (0, 1))
                    store_outputs(sp, h - 1, range(half, NT - 2))
                    load_weights(sp, h + 1, (2, 3))
                    store_outputs(sp, h - 1, range(NT - 2, NT))
                    store_outputs(sp, h, range(half))
                store_outputs(sp, H - 2, range(half, NT - 2))
                sp.wait_ge(proj_half, H * 2 * NT)
                for kt in range(KT):
                    sp.dma_start(w_out_raw[:, kt, :], w_out[kt * P:(kt + 1) * P, :])\
                      .then_inc(w_out_loaded, 16)
                store_outputs(sp, H - 2, range(NT - 2, NT))
                store_outputs(sp, H - 1, range(NT))
                for par in range(2):
                    sp.wait_ge(o_stored[par], 16 * (H * NT // 2 + 1))

            @block.gpsimd
            def _(pool):
                run_heads(pool, lambda h, kind: pool_head(pool, h, kind))

            @block.scalar
            def _(act):
                run_heads(act, lambda h, kind: act_head(act, h, kind))

            @block.vector
            def _(dve):
                run_heads(dve, lambda h, kind: dve_head(dve, h, kind))

            @block.tensor
            def _(pe):
                run_heads(pe, lambda h, kind: pe_head(pe, h, kind))


def w1_piece(w1, n):
    return w1.rearrange("(kt p) f -> p kt f", p=P)[:, :, n * P:(n + 1) * P]


def output_step(nc, x, o_dram, sub_g, norm2_g, h_dram, u2_dram, w_hi, w_lo, u4,
                w1, w1_raw, w1_loaded):
    with ExitStack() as ctx:
        def sb(name, shape, dt=F32):
            return ctx.enter_context(nc.sbuf_tensor(name, shape, dt))

        def sem(name):
            return ctx.enter_context(nc.semaphore(name))

        o_in = sb("o_in", [P, 2, D])
        x_in = sb("x_res", [P, 2, D])
        ot_hi = sb("ot_hi", [P, 2, D], F32R)
        ot_lo = sb("ot_lo", [P, 2, D], F32R)
        h_out = sb("h_out", [P, 2, D])
        h_ss = sb("h_ss", [P, 2])
        h_var = sb("h_var", [P, 2])
        h_rs = sb("h_rs", [P, 2])
        u_nat = sb("u2_nat", [P, 2, D])
        u_hi = sb("u2_hi_tile", [P, 2, D], F32R)
        u_lo = sb("u2_lo_tile", [P, 2, D], F32R)
        ident = sb("ident3", [P, P])
        minus_half = sb("minus_half3", [P, 1])
        eps = sb("eps3", [P, 1])
        g_raw = sb("sub_g_raw", [P, 1])
        g_o = sb("sub_g_col", [P, 1])
        g2_row = sb("g2_row", [P, D])
        o_turn = ctx.enter_context(nc.psum_tensor("o_turn", [P, D], F32))
        u_turn = ctx.enter_context(nc.psum_tensor("u_turn", [P, D], F32))
        product = ctx.enter_context(nc.psum_tensor("product", [P, 2, D], F32))

        gain_loaded, g2_loaded, ident_set, g_set = (
            sem("gain_loaded"), sem("g2_loaded"), sem("ident3_set"), sem("g3_set"))
        o_loaded = [sem("o_loaded0"), sem("o_loaded1")]
        x_loaded = [sem("xr_loaded0"), sem("xr_loaded1")]
        o_turned, ot_hi_set, ot_lo_set = sem("o_turned"), sem("ot_hi_set"), sem("ot_lo_set")
        multiplied, h_set, h_squared = sem("multiplied"), sem("h_set"), sem("h_squared")
        h_var_set, h_rs_set, u_normed, u_turned = (
            sem("h_var_set"), sem("h_rs_set"), sem("u2_normed"), sem("u2_turned"))
        u_hi_set, u_lo_set = sem("u2_hi_set"), sem("u2_lo_set")
        h_stored = [sem("h_stored0"), sem("h_stored1")]
        u_stored = [sem("u2_stored0"), sem("u2_stored1")]

        LAST = NT // 2 - 1

        def rounds(engine, tile):
            for r in range(CT // 2 + 1):
                for q in range(2):
                    tile(r, q)
            with engine.Fori(CT // 2 + 1, LAST) as r:
                for q in range(2):
                    tile(r, q)
            for q in range(2):
                tile(LAST, q)

        def static(r, value):
            return isinstance(r, int) and r == value

        def kept(r, q):
            return isinstance(r, int) and r * 2 + q < CT

        def split_target(u, a, r, q):
            return u4[:, a, r * 2 + q, :] if kept(r, q) else u[:, q, :]

        def before(r, q):
            return (r, 0) if q else (r - 1, 1)

        def after(r, q):
            return (r + 1, 0) if q else (r, 1)

        with nc.Block() as block:
            @block.sync
            def _(sp):
                def rows(r, q):
                    row = (r * 2 + q) * P
                    return bass.ds(row if isinstance(row, int) else sp.snap(row), P)

                def load(r, q, at):
                    if not static(r, 0):
                        sp.wait_ge(o_turned, r * 2 + q - 1)
                    sp.dma_start(o_in[:, q, :], o_dram[at, :]).then_inc(o_loaded[q], 16)
                    sp.dma_start(x_in[:, q, :], x[at, :]).then_inc(x_loaded[q], 16)

                def store_u(r, q):
                    if kept(r, q):
                        return
                    row = (r * 2 + q - CT) * P
                    at = bass.ds(row if isinstance(row, int) else sp.snap(row), P)
                    sp.wait_ge(u_lo_set, r * 2 + q + 1)
                    sp.dma_start(u2_dram[0, at, :], u_hi[:, q, :].bitcast(F32)).then_inc(u_stored[q], 16)
                    sp.dma_start(u2_dram[1, at, :], u_lo[:, q, :].bitcast(F32)).then_inc(u_stored[q], 16)

                def tile(r, q):
                    ats = {"this": rows(r, q), "next": rows(r + 1, q)}
                    if not (static(r, 0) and q == 0):
                        store_u(*before(r, q))
                    sp.wait_ge(h_set, r * 2 + q + 1)
                    sp.dma_start(h_dram[ats["this"], :], h_out[:, q, :]).then_inc(h_stored[q], 16)
                    if not static(r, LAST):
                        load(r + 1, q, ats["next"])

                with nc.allow_non_contiguous_dma("a gain, once"):
                    sp.dma_start(g_raw[:, :], sub_g.rearrange("a d -> d a")).then_inc(gain_loaded, 16)
                load(0, 0, rows(0, 0))
                load(0, 1, rows(0, 1))
                sp.dma_start(g2_row[:, :], norm2_g.to_broadcast([P, D])).then_inc(g2_loaded, 16)
                for n in range(2):
                    sp.dma_start(w1_raw[:, n, :, :], w1_piece(w1, n)).then_inc(w1_loaded[n], 16)
                rounds(sp, tile)
                store_u(LAST, 1)
                for q in range(2):
                    sp.wait_ge(h_stored[q], 16 * NT // 2)
                    sp.wait_ge(u_stored[q], 32 * ((NT - CT) // 2 + 1))

            @block.gpsimd
            def _(pool):
                pool.memset(ident[:, :], 0.0).then_inc(ident_set, 1)
                pool.wait_ge(ident_set, 1)
                pool.affine_select(out=ident[:, :], in_=ident[:, :], compare_op=ALU.not_equal, fill=1.0,
                                   base=0, pattern=[[-1, P]], channel_multiplier=1).then_inc(ident_set, 1)
                pool.memset(minus_half[:, :], -0.5).then_inc(ident_set, 1)
                pool.memset(eps[:, :], EPS).then_inc(ident_set, 1)
                pool.wait_ge(ident_set, 4)

                def tile(r, q):
                    n = r * 2 + q
                    pool.wait_ge(h_squared, n + 1)
                    pool.tensor_tensor(h_var[:, q:q + 1], h_ss[:, q:q + 1], eps[:, :], ALU.add)\
                        .then_inc(h_var_set, 1)
                    pool.wait_ge(h_var_set, n + 1)
                    pool.tensor_tensor(h_rs[:, q:q + 1], h_var[:, q:q + 1], minus_half[:, :], ALU.pow)\
                        .then_inc(h_rs_set, 1)

                rounds(pool, tile)

            @block.scalar
            def _(act):
                def split_o(r, q):
                    n = r * 2 + q
                    act.wait_ge(o_turned, n + 1)
                    if not static(r, 0):
                        act.wait_ge(multiplied, 2 * (n - 1))
                    act.activation(ot_hi[:, q, :], o_turn[:, :], ACT.Copy, scale=g_o[:, :]).then_inc(ot_hi_set, 1)

                def split_u(r, q):
                    act.wait_ge(u_turned, r * 2 + q + 1)
                    if not kept(r, q):
                        act.wait_ge(u_stored[q], 32 * (r - CT // 2 + 1))
                    act.activation(split_target(u_hi, 0, r, q), u_turn[:, :], ACT.Copy).then_inc(u_hi_set, 1)

                def tile(r, q):
                    n = r * 2 + q
                    if not (static(r, 0) and q == 0):
                        split_u(*before(r, q))
                    if not (static(r, LAST) and q == 1):
                        split_o(*after(r, q))
                    act.wait_ge(h_set, n + 1)
                    if not static(r, 0):
                        act.wait_ge(h_var_set, n - 1)
                        act.wait_ge(u_turned, n - 1)
                    act.activation(u_nat[:, q, :], h_out[:, q, :], ACT.Square, scale=D ** -0.5,
                                   accum_out=h_ss[:, q:q + 1])\
                       .then_inc(h_squared, 1)

                act.wait_ge(gain_loaded, 16)
                act.activation(g_o[:, :], g_raw[:, :], ACT.Copy, scale=1.0 - LAMBDA_INIT).then_inc(g_set, 1)
                act.wait_ge(g_set, 1)
                split_o(0, 0)
                rounds(act, tile)
                split_u(LAST, 1)

            @block.vector
            def _(dve):
                def split_o(r, q):
                    n = r * 2 + q
                    dve.wait_ge(ot_hi_set, n + 1)
                    dve.scalar_tensor_tensor(ot_lo[:, q, :], o_turn[:, :], g_o[:, :], ot_hi[:, q, :].bitcast(F32),
                                             ALU.mult, ALU.subtract).then_inc(ot_lo_set, 1)

                def norm_u(r, q):
                    n = r * 2 + q
                    dve.wait_ge(h_rs_set, n + 1)
                    dve.scalar_tensor_tensor(u_nat[:, q, :], h_out[:, q, :], h_rs[:, q:q + 1], g2_row[:, :],
                                             ALU.mult, ALU.mult).then_inc(u_normed, 1)

                def split_u(r, q):
                    dve.wait_ge(u_hi_set, r * 2 + q + 1)
                    dve.tensor_tensor(split_target(u_lo, 1, r, q), u_turn[:, :],
                                      split_target(u_hi, 0, r, q).bitcast(F32), ALU.subtract)\
                       .then_inc(u_lo_set, 1)

                def tile(r, q):
                    n = r * 2 + q
                    if not (static(r, 0) and q == 0):
                        norm_u(*before(r, q))
                        split_u(*before(r, q))
                    if not (static(r, LAST) and q == 1):
                        split_o(*after(r, q))
                    dve.wait_ge(multiplied, 2 * n + 2)
                    dve.wait_ge(x_loaded[q], 16 * (r + 1))
                    dve.wait_ge(h_stored[q], 16 * r)
                    if not static(r, 0):
                        dve.wait_ge(u_normed, n - 1)
                    dve.tensor_tensor(h_out[:, q, :], product[:, q, :], x_in[:, q, :], ALU.add).then_inc(h_set, 1)

                for q in range(2):
                    dve.memset(u_lo[:, q, 0:1].bitcast(F32), 0.0).then_inc(u_stored[q], 32)
                split_o(0, 0)
                dve.wait_ge(g2_loaded, 16)
                rounds(dve, tile)
                norm_u(LAST, 1)
                split_u(LAST, 1)

            @block.tensor
            def _(pe):
                def turn_o(r, q):
                    n = r * 2 + q
                    pe.wait_ge(o_loaded[q], 16 * (r + 1))
                    pe.wait_ge(ot_lo_set, n)
                    for kt in range(KT):
                        last = pe.transpose(o_turn[:, kt * P:(kt + 1) * P], o_in[:, q, kt * P:(kt + 1) * P],
                                            ident[:, :])
                    last.then_inc(o_turned, 1)

                def turn_u(r, q):
                    n = r * 2 + q
                    pe.wait_ge(u_normed, n + 1)
                    pe.wait_ge(u_lo_set, n)
                    for kt in range(KT):
                        last = pe.transpose(u_turn[:, kt * P:(kt + 1) * P], u_nat[:, q, kt * P:(kt + 1) * P],
                                            ident[:, :])
                    last.then_inc(u_turned, 1)

                def half(r, q, dh):
                    cols = slice(dh * BANK, (dh + 1) * BANK)
                    if dh == 0:
                        pe.wait_ge(ot_lo_set, r * 2 + q + 1)
                        if not static(r, 0):
                            pe.wait_ge(h_set, r * 2 + q - 1)
                    for kt in range(KT):
                        for a, w in ((ot_hi, w_hi), (ot_hi, w_lo), (ot_lo, w_hi)):
                            last = pe.matmul(product[:, q, cols], a[:, q, kt * P:(kt + 1) * P], w[:, kt, cols],
                                             start=(kt == 0 and a is ot_hi and w is w_hi),
                                             stop=(kt == KT - 1 and a is ot_lo))
                    last.then_inc(multiplied, 1)

                def tile(r, q):
                    half(r, q, 0)
                    if not (static(r, 0) and q == 0):
                        turn_u(*before(r, q))
                    if not (static(r, LAST) and q == 1):
                        turn_o(*after(r, q))
                    half(r, q, 1)

                pe.wait_ge(ident_set, 4)
                turn_o(0, 0)
                rounds(pe, tile)
                turn_u(LAST, 1)


def mlp_step(nc, h_dram, u2_dram, w1, w2, out, y, hid_hi, hid_lo, u4, w1_raw, w1_loaded):
    with ExitStack() as ctx:
        def sb(name, shape, dt=F32):
            return ctx.enter_context(nc.sbuf_tensor(name, shape, dt))

        def sem(name):
            return ctx.enter_context(nc.semaphore(name))

        NB = DFF // (FT * P)
        NH = CT * P // BANK
        E = FT * NH
        G = 2 * CT
        W1N, W2N = FT, 4

        u_hi = u4[:, 0, :, :].rearrange("p t (k r) -> p t k r", k=KT)
        u_lo = u4[:, 1, :, :].rearrange("p t (k r) -> p t k r", k=KT)
        w1_hi = sb("w1_hi", [P, 2, KT, P], F32R)
        w1_lo = sb("w1_lo", [P, 2, KT, P], F32R)
        w2_raw = sb("w2_raw", [P, 2, 2, BANK])
        w2_hi = sb("w2_hi", [P, 2, FT, BANK], F32R)
        w2_lo = sb("w2_lo", [P, 2, FT, BANK], F32R)
        relu = sb("relu", [P, 2, BANK])
        relu_sq = sb("relu_sq", [P, 2, BANK])
        banks = ctx.enter_context(nc.psum_tensor("banks", [P, 8, BANK], F32))

        u_loaded = [sem(f"u4_loaded{n}") for n in range(NH)]
        y_loaded, y_stored = sem("y_loaded"), sem("y_stored")
        w2_loaded = [sem("w2_loaded0"), sem("w2_loaded1")]
        w1_hi_set, w1_lo_set, w2_hi_set, w2_lo_set = (
            sem("w1_hi_set"), sem("w1_lo_set"), sem("w2_hi_set"), sem("w2_lo_set"))
        hid_done, relu_set, sq_set, hid_hi_set, hid_lo_set = (
            sem("hid_done"), sem("relu_set"), sem("sq_set"), sem("hid_hi_set"), sem("hid_lo_set"))
        y_done, y_added = sem("y_done"), sem("y_added")

        w1_view = w1.rearrange("(kt p) f -> p kt f", p=P)
        w2_view = w2.rearrange("(ft p) d -> p ft d", p=P)
        u_view = u2_dram.rearrange("a (t p) d -> a p t d", p=P)
        h_view = h_dram.rearrange("(t p) d -> p t d", p=P)

        def blocks(engine, block):
            for c in range(CHUNKS):
                block(0, c * NB, c)
                with engine.Fori(1, NB) as b:
                    block(b, b + c * NB, None)

        def static(it, value):
            return isinstance(it, int) and it == value

        with nc.Block() as block:
            @block.sync
            def _(sp):
                def at(value):
                    return value if isinstance(value, int) else sp.snap(value)

                def loads(b, it, chunk):
                    w1_cols = [bass.ds(at(b * (FT * P) + n * P), P) for n in range(FT)]
                    w2_tiles = [bass.ds(at(b * FT + f), 2) for f in (0, 2)]
                    for n in range(FT):
                        if not (static(it, 0) and n < 2):
                            sp.wait_ge(w1_lo_set, it * W1N + n - 1)
                        if not (static(it, 0) and n < 2):
                            sp.dma_start(w1_raw[:, n % 2, :, :], w1_view[:, :, w1_cols[n]])\
                              .then_inc(w1_loaded[n % 2], 16)
                        if not (static(it, 0) and n < 2):
                            sp.wait_ge(w2_lo_set, it * W2N + n - 1)
                        dh = n // 2
                        sp.dma_start(w2_raw[:, n % 2, :, :],
                                     w2_view[:, w2_tiles[n % 2], dh * BANK:(dh + 1) * BANK])\
                          .then_inc(w2_loaded[n % 2], 16)

                blocks(sp, loads)

            @block.gpsimd
            def _(pool):
                def split_w1(it, n):
                    pool.wait_ge(w1_hi_set, it * W1N + n + 1)
                    pool.tensor_tensor(w1_lo[:, n % 2, :, :], w1_raw[:, n % 2, :, :],
                                       w1_hi[:, n % 2, :, :].bitcast(F32), ALU.subtract).then_inc(w1_lo_set, 1)

                def body(b, it, chunk):
                    split_w1(it, 0)
                    split_w1(it, 1)
                    for j in range(FT):
                        for n in range(NH):
                            pool.wait_ge(hid_hi_set, it * E + j * NH + n + 1)
                            rows = slice(n * BANK, (n + 1) * BANK)
                            pool.tensor_tensor(hid_lo[:, j, rows], relu_sq[:, n, :],
                                               hid_hi[:, j, rows].bitcast(F32), ALU.subtract)\
                                .then_inc(hid_lo_set, 1)
                        if j + 2 < FT:
                            split_w1(it, j + 2)

                blocks(pool, body)

            @block.scalar
            def _(act):
                def load_u(c):
                    for n in range(NH):
                        tiles = slice(n * TPB, (n + 1) * TPB)
                        for a, u in enumerate((u_hi, u_lo)):
                            act.dma_start(u[:, tiles, :, :].rearrange("p t k r -> p t (k r)").bitcast(F32),
                                          u_view[a, :, (c - 1) * CT + n * TPB:(c - 1) * CT + (n + 1) * TPB, :])\
                               .then_inc(u_loaded[n], 16)

                def store_y(c):
                    for t in range(CT):
                        act.wait_ge(y_added, (c + 1) * NB * G - CT + t + 1)
                        row = (c * CT + t) * P
                        act.dma_start(out[row:row + P, :], y[:, t, :]).then_inc(y_stored, 16)

                def split_w1(it, n):
                    act.wait_ge(w1_loaded[n % 2], 16 * (it * 2 + n // 2 + 1))
                    if n >= 2:
                        act.wait_ge(hid_done, it * E + (n - 1) * NH)
                    else:
                        act.wait_ge(hid_done, it * E)
                    act.activation(w1_hi[:, n % 2, :, :], w1_raw[:, n % 2, :, :], ACT.Copy).then_inc(w1_hi_set, 1)

                def body(b, it, chunk):
                    if chunk:
                        act.wait_ge(hid_done, it * E)
                        load_u(chunk)
                    split_w1(it, 0)
                    split_w1(it, 1)
                    if chunk is not None:
                        if chunk:
                            store_y(chunk - 1)
                            act.wait_ge(y_stored, 16 * CT * chunk)
                        act.dma_start(y[:, :, :], h_view[:, chunk * CT:(chunk + 1) * CT, :]).then_inc(y_loaded, 16)
                    for j in range(FT):
                        for n in range(NH):
                            e = it * E + j * NH + n
                            act.wait_ge(hid_done, e + 1)
                            act.activation(relu[:, n, :], banks[:, j * NH + n, :], ACT.Relu).then_inc(relu_set, 1)
                            act.wait_ge(sq_set, e + 1)
                            act.wait_ge(y_done, it * G)
                            act.activation(hid_hi[:, j, n * BANK:(n + 1) * BANK], relu_sq[:, n, :], ACT.Copy)\
                               .then_inc(hid_hi_set, 1)
                        if j + 2 < FT:
                            split_w1(it, j + 2)
                        act.wait_ge(w2_loaded[j % 2], 16 * (it * 2 + j // 2 + 1))
                        act.activation(w2_hi[:, j // 2, (j % 2) * 2:(j % 2) * 2 + 2, :], w2_raw[:, j % 2, :, :],
                                       ACT.Copy).then_inc(w2_hi_set, 1)

                blocks(act, body)
                store_y(CHUNKS - 1)
                act.wait_ge(y_stored, 16 * NT)

            @block.vector
            def _(dve):
                def body(b, it, chunk):
                    for j in range(FT):
                        for n in range(NH):
                            e = it * E + j * NH + n
                            dve.wait_ge(relu_set, e + 1)
                            if j * NH + n >= 2:
                                dve.wait_ge(hid_lo_set, e - 1)
                            else:
                                dve.wait_ge(hid_lo_set, it * E)
                            dve.scalar_tensor_tensor(relu_sq[:, n, :], banks[:, j * NH + n, :], 0.0, relu[:, n, :],
                                                     ALU.max, ALU.mult).then_inc(sq_set, 1)
                        dve.wait_ge(w2_hi_set, it * W2N + j + 1)
                        piece = (slice(None), j // 2, slice((j % 2) * 2, (j % 2) * 2 + 2))
                        dve.tensor_tensor(w2_lo[piece], w2_raw[:, j % 2, :, :], w2_hi[piece].bitcast(F32),
                                          ALU.subtract).then_inc(w2_lo_set, 1)
                    if chunk is not None:
                        dve.wait_ge(y_loaded, 16 * (chunk + 1))
                    for g in range(G):
                        dh, t = g // CT, g % CT
                        part = y[:, t, dh * BANK:(dh + 1) * BANK]
                        dve.wait_ge(y_done, it * G + g + 1)
                        dve.wait_ge(y_added, it * G + g - (G - 1) if not isinstance(it, int) else
                                    max(it * G + g - (G - 1), 0))
                        dve.tensor_tensor(part, banks[:, g % 8, :], part, ALU.add).then_inc(y_added, 1)

                blocks(dve, body)

            @block.tensor
            def _(pe):
                def body(b, it, chunk):
                    for j in range(FT):
                        pe.wait_ge(w1_lo_set, it * W1N + j + 1)
                        for n in range(NH):
                            e = j * NH + n
                            if chunk and j == 0:
                                pe.wait_ge(u_loaded[n], 32 * chunk)
                            if not static(it, 0):
                                pe.wait_ge(y_added, it * G - 8 + e + 1)
                            for kt in range(KT):
                                for w, u in ((w1_hi, u_hi), (w1_hi, u_lo), (w1_lo, u_hi)):
                                    last = pe.matmul(banks[:, e, :], w[:, j % 2, kt, :],
                                                     u[:, n * TPB:(n + 1) * TPB, kt, :],
                                                     start=(kt == 0 and w is w1_hi and u is u_hi),
                                                     stop=(kt == KT - 1 and w is w1_lo))
                            last.then_inc(hid_done, 1)
                    for g in range(G):
                        dh, t = g // CT, g % CT
                        if t == 0:
                            pe.wait_ge(w2_lo_set, it * W2N + 2 * dh + 2)
                        if dh == 0 and t % TPB == 0:
                            pe.wait_ge(hid_lo_set, it * E + E - NH + t // TPB + 1)
                        if g < 8:
                            pe.wait_ge(sq_set, it * E + g + 1)
                        else:
                            pe.wait_ge(y_added, it * G + g - 8 + 1)
                        for j in range(FT):
                            for a, w in ((hid_hi, w2_hi), (hid_hi, w2_lo), (hid_lo, w2_hi)):
                                last = pe.matmul(banks[:, g % 8, :], a[:, j, t * P:(t + 1) * P], w[:, dh, j, :],
                                                 start=(j == 0 and a is hid_hi and w is w2_hi),
                                                 stop=(j == FT - 1 and a is hid_lo))
                        last.then_inc(y_done, 1)

                blocks(pe, body)


def build_program(nc, x, norm1_g, norm2_g, a_w_in, a_q_norm_g, a_k_norm_g, a_lambda_q1, a_lambda_k1,
                  a_lambda_q2, a_lambda_k2, a_subln_g, a_w_out, mlp_w1, mlp_w2, out):
    scratch = nc.dram_tensor("rows_scratch", [2, S, D], F32).ap()
    h_dram, o_dram = scratch[0], scratch[1]
    u2_dram = nc.dram_tensor("u2_scratch", [2, S - CT * P, D], F32).ap()
    base, half = -(-nc.sbuf_base // 32) * 32, KT * D * 4
    with nc.sbuf_tensor("place", [P, 2 * half // 4], F32):
        def at(name, shape, dt, offset):
            return nc.alloc_sbuf_tensor_at(name, shape, dt, offset=base + offset)

        u_t = at("u_t", [P, NT, KT, P], F32, 0)
        w_out_hi, w_out_lo = at("w_out_hi", [P, KT, D], F32R, 0), at("w_out_lo", [P, KT, D], F32R, half)
        w_out_raw = at("w_out_raw", [P, KT, D], F32, half)
        y = at("y", [P, CT, D], F32, 0)
        hid_hi = at("hid_hi", [P, FT, CT * P], F32R, half)
        hid_lo = at("hid_lo", [P, FT, CT * P], F32R, half + FT * CT * P * 4)
        attention_steps(nc, x[0], norm1_g, a_w_in[0], a_q_norm_g, a_k_norm_g,
                        [a_lambda_q1, a_lambda_k1, a_lambda_q2, a_lambda_k2], a_w_out[0], o_dram,
                        u_t, w_out_raw, w_out_hi, w_out_lo)
        with (nc.sbuf_tensor("u4", [P, 2, CT, D], F32R) as u4,
              nc.sbuf_tensor("w1_raw", [P, 2, KT, P], F32) as w1_raw,
              nc.semaphore("w1_loaded0") as loaded0, nc.semaphore("w1_loaded1") as loaded1):
            output_step(nc, x[0], o_dram, a_subln_g, norm2_g, h_dram, u2_dram, w_out_hi, w_out_lo, u4,
                        mlp_w1[0], w1_raw, [loaded0, loaded1])
            mlp_step(nc, h_dram, u2_dram, mlp_w1[0], mlp_w2[0], out[0], y, hid_hi, hid_lo, u4,
                     w1_raw, [loaded0, loaded1])


_INS = ["x", "norm1_g", "norm2_g", "a_w_in", "a_q_norm_g", "a_k_norm_g", "a_lambda_q1", "a_lambda_k1",
        "a_lambda_q2", "a_lambda_k2", "a_subln_g", "a_w_out", "mlp_w1", "mlp_w2"]


def kernel(**inputs):
    import numpy as _np
    import concourse.bacc as _bacc
    from concourse.bass_utils import run_bass_kernel_spmd as _run

    nc = _bacc.Bacc("TRN2", target_bir_lowering=False, num_devices=1)
    arrays, args = {}, []
    for name in _INS:
        a = _np.ascontiguousarray(inputs[name])
        arrays[f"in_{name}"] = a
        args.append(nc.dram_tensor(f"in_{name}", a.shape, mybir.dt.from_np(a.dtype), kind="ExternalInput").ap())
    out = nc.dram_tensor("out", (1, S, D), F32, kind="ExternalOutput").ap()
    build_program(nc, *args, out)
    r = _run(nc, [arrays], core_ids=[0])
    return r.results[0]["out"]
```
